# Optimizing a Trainium2 kernel written in Bass

```python
import math
import jax, jax.numpy as jnp
from jax import lax
import numpy as np

D_MODEL = 2048
BATCH = 1
SEQ = 256
DEPTH = 1

CHUNK = 64
HEAD_DIM = 64
HA = 16
KVA = 2
GA = HA // KVA
WINDOW = 128
WIN_PREV = WINDOW // CHUNK - 1
HB = 16
BAND_PREV = 8
REL_CLIP = 256
REL_TABLE = REL_CLIP + CHUNK
T5_BUCKETS = 32
T5_MAX_DISTANCE = 64
QA_W = HA * HEAD_DIM
KVA_W = KVA * HEAD_DIM
QB_W = HB * HEAD_DIM
SPLITS = [QA_W, QA_W + KVA_W, QA_W + 2 * KVA_W, QA_W + 2 * KVA_W + QB_W,
          QA_W + 2 * KVA_W + 2 * QB_W, QA_W + 2 * KVA_W + 3 * QB_W,
          QA_W + 2 * KVA_W + 3 * QB_W + D_MODEL]
IN_W = QA_W + 2 * KVA_W + 3 * QB_W + 2 * D_MODEL
N_EXPERTS = 16
N_GROUPS = 4
EPG = N_EXPERTS // N_GROUPS
TOP_K = 2
D_FF = D_MODEL // 2
PLE_DIM = 256
ALPHA = (2.0 * DEPTH) ** 0.25
BETA = (8.0 * DEPTH) ** -0.25
LN_EPS = 1e-5
NEG_INF = -1e30

kernel_name = "hybrid_chunk_causal_gated_moe_block"

def layer_norm(x, g, b):
    xf = x.astype(jnp.float32)
    mu = xf.mean(-1, keepdims=True)
    var = jnp.square(xf - mu).mean(-1, keepdims=True)
    return ((xf - mu) * lax.rsqrt(var + LN_EPS) * g.astype(jnp.float32)
            + b.astype(jnp.float32)).astype(x.dtype)

def band_rel(n_prev):
    L = (n_prev + 1) * CHUNK
    return np.arange(L)[None, :] - n_prev * CHUNK - np.arange(CHUNK)[:, None]

def band_valid(nc, n_prev):
    key_chunk = (np.arange(nc)[:, None] - n_prev
                 + np.repeat(np.arange(n_prev + 1), CHUNK)[None, :])
    return key_chunk >= 0

def t5_bucket(rel):
    nb = T5_BUCKETS // 2
    ret = (rel > 0).astype(np.int32) * nb
    n = np.abs(rel)
    max_exact = nb // 2
    large = max_exact + (np.log(np.maximum(n, 1).astype(np.float32) / max_exact)
                         / np.log(T5_MAX_DISTANCE / max_exact)
                         * (nb - max_exact)).astype(np.int32)
    large = np.minimum(large, nb - 1)
    return ret + np.where(n < max_exact, n, large)

def chunk_band(t, n_prev):
    B, S = t.shape[:2]
    nc = S // CHUNK
    tc = t.reshape((B, nc, CHUNK) + t.shape[2:])
    pad = jnp.zeros((B, n_prev) + tc.shape[2:], t.dtype)
    tp = jnp.concatenate([pad, tc], axis=1)
    idx = np.arange(nc)[:, None] + np.arange(n_prev + 1)[None, :]
    band = tp[:, idx]
    return band.reshape((B, nc, (n_prev + 1) * CHUNK) + t.shape[2:])

def band_attention(q, k, v, n_prev, bias, sink):
    B, S, KV, G, hd = q.shape
    nc = S // CHUNK
    qc = q.reshape(B, nc, CHUNK, KV, G, hd)
    kb = chunk_band(k, n_prev)
    vb = chunk_band(v, n_prev)
    logits = jnp.einsum('bnqkgd,bnjkd->bnkgqj', qc, kb,
                        preferred_element_type=jnp.float32) * (hd ** -0.5)
    logits = logits + bias.astype(jnp.float32)
    valid = band_valid(nc, n_prev)
    logits = jnp.where(valid[None, :, None, None, None, :], logits, NEG_INF)
    if sink is None:
        probs = jax.nn.softmax(logits, axis=-1)
    else:
        s = sink.astype(jnp.float32)[None, None, :, :, None, None]
        m = jnp.maximum(logits.max(-1, keepdims=True), s)
        e = jnp.exp(logits - m)
        probs = e / (e.sum(-1, keepdims=True) + jnp.exp(s - m))
    out = jnp.einsum('bnkgqj,bnjkd->bnqkgd', probs.astype(v.dtype), vb)
    return out.reshape(B, S, KV * G * hd)

def grouped_top2_combine(xt, w_router, b_router):
    T = xt.shape[0]
    logits = jnp.einsum('td,de->te', xt, w_router, preferred_element_type=jnp.float32)
    probs = jax.nn.softmax(logits, axis=-1)
    sel = (probs + b_router.astype(jnp.float32)).reshape(T, N_GROUPS, EPG)
    grp_score = lax.top_k(sel, 2)[0].sum(-1)
    g = jnp.argmax(grp_score, axis=-1)
    in_grp = jnp.take_along_axis(sel, g[:, None, None], axis=1)[:, 0]
    _, loc = lax.top_k(in_grp, TOP_K)
    idx = g[:, None] * EPG + loc
    w = jnp.take_along_axis(probs, idx, axis=-1)
    w = w / w.sum(-1, keepdims=True)
    return jnp.sum(jax.nn.one_hot(idx, N_EXPERTS, dtype=jnp.float32) * w[..., None], axis=1)

def setup_inputs(seed: int = 0) -> dict:
    key = jax.random.key(seed)
    ks = jax.random.split(key, 32)

    def nrm(k, shape, scale):
        return jax.random.normal(k, shape, jnp.float32) * scale

    s_d = D_MODEL ** -0.5
    x = nrm(ks[0], (BATCH, SEQ, D_MODEL), 1.0)
    p = nrm(ks[1], (DEPTH, BATCH, SEQ, PLE_DIM), 1.0)
    w_in = jnp.concatenate([
        nrm(ks[2], (DEPTH, D_MODEL, QA_W), s_d),
        nrm(ks[3], (DEPTH, D_MODEL, KVA_W), s_d),
        nrm(ks[4], (DEPTH, D_MODEL, KVA_W), s_d * BETA),
        nrm(ks[5], (DEPTH, D_MODEL, QB_W), s_d),
        nrm(ks[6], (DEPTH, D_MODEL, QB_W), s_d),
        nrm(ks[7], (DEPTH, D_MODEL, QB_W), s_d * BETA),
        nrm(ks[8], (DEPTH, D_MODEL, 2 * D_MODEL), s_d),
    ], axis=-1)
    w_pa = nrm(ks[9], (DEPTH, QA_W, D_MODEL), QA_W ** -0.5 * BETA)
    w_pb = nrm(ks[10], (DEPTH, QB_W, D_MODEL), QB_W ** -0.5 * BETA)
    w_o = nrm(ks[11], (DEPTH, D_MODEL, D_MODEL), s_d * BETA)
    attn_sinks = nrm(ks[12], (DEPTH, HA), 1.0)
    relb_table = nrm(ks[13], (DEPTH, REL_TABLE, HB), 0.5)
    ln1_g = 1.0 + nrm(ks[14], (DEPTH, D_MODEL), 0.02)
    ln1_b = nrm(ks[15], (DEPTH, D_MODEL), 0.02)
    w_router = nrm(ks[16], (D_MODEL, N_EXPERTS), s_d)
    b_router = nrm(ks[17], (N_EXPERTS,), 0.01)
    w1 = nrm(ks[18], (DEPTH, N_EXPERTS, D_MODEL, D_FF), s_d)
    w3 = nrm(ks[19], (DEPTH, N_EXPERTS, D_MODEL, D_FF), s_d)
    w2 = nrm(ks[20], (DEPTH, N_EXPERTS, D_FF, D_MODEL), D_FF ** -0.5 * BETA)
    w_ple = nrm(ks[21], (DEPTH, PLE_DIM, D_MODEL), PLE_DIM ** -0.5 * BETA)
    w_ple_gate = nrm(ks[22], (DEPTH, D_MODEL, D_MODEL), s_d)
    ln2_g = 1.0 + nrm(ks[23], (DEPTH, D_MODEL), 0.02)
    ln2_b = nrm(ks[24], (DEPTH, D_MODEL), 0.02)
    t5_table = nrm(ks[25], (T5_BUCKETS, HA), 0.5)
    return {"x": x, "p": p, "w_in": w_in, "w_pa": w_pa, "w_pb": w_pb, "w_o": w_o,
            "attn_sinks": attn_sinks, "relb_table": relb_table, "ln1_g": ln1_g,
            "ln1_b": ln1_b, "w_router": w_router, "b_router": b_router, "w1": w1,
            "w3": w3, "w2": w2, "w_ple": w_ple, "w_ple_gate": w_ple_gate,
            "ln2_g": ln2_g, "ln2_b": ln2_b, "t5_table": t5_table}

def reference(x, p, w_in, w_pa, w_pb, w_o, attn_sinks, relb_table, ln1_g, ln1_b,
              w_router, b_router, w1, w3, w2, w_ple, w_ple_gate, ln2_g, ln2_b, t5_table):
    B, S, D = x.shape
    T = B * S
    idx_a = t5_bucket(band_rel(WIN_PREV))
    bias_a = t5_table[idx_a].transpose(2, 0, 1).reshape(KVA, GA, CHUNK, -1)
    idx_b = np.clip(band_rel(BAND_PREV), -REL_CLIP, CHUNK - 1) + REL_CLIP

    for i in range(DEPTH):
        h = x @ w_in[i]
        qa, ka, va, qb, kb, vb, ga, gb = jnp.split(h, SPLITS, axis=-1)
        ya = band_attention(qa.reshape(B, S, KVA, GA, HEAD_DIM),
                            ka.reshape(B, S, KVA, HEAD_DIM),
                            va.reshape(B, S, KVA, HEAD_DIM),
                            WIN_PREV, bias_a, attn_sinks[i].reshape(KVA, GA))
        bias_b = relb_table[i][idx_b].transpose(2, 0, 1)[:, None]
        yb = band_attention(qb.reshape(B, S, HB, 1, HEAD_DIM),
                            kb.reshape(B, S, HB, HEAD_DIM),
                            vb.reshape(B, S, HB, HEAD_DIM),
                            BAND_PREV, bias_b, None)
        merged = jax.nn.sigmoid(ga) * (ya @ w_pa[i]) + jax.nn.sigmoid(gb) * (yb @ w_pb[i])
        x = layer_norm(ALPHA * x + merged @ w_o[i], ln1_g[i], ln1_b[i])

        xt = x.reshape(T, D)
        combine = grouped_top2_combine(xt, w_router, b_router).astype(x.dtype)
        moe = jnp.zeros_like(xt)
        for e in range(N_EXPERTS):
            he = jax.nn.silu(xt @ w1[i, e]) * (xt @ w3[i, e])
            moe = moe + combine[:, e:e + 1] * (he @ w2[i, e])
        ple = jax.nn.sigmoid(x @ w_ple_gate[i]) * (p[i] @ w_ple[i])
        x = layer_norm(ALPHA * x + moe.reshape(B, S, D) + ple, ln2_g[i], ln2_b[i])
    return x


_drawn_inputs = setup_inputs


def setup_inputs(seed=0):
    import zlib

    import numpy as np

    out = dict(_drawn_inputs(seed))
    spreads = {}
    factors = {'w_pb': 3.198,
     'attn_sinks': 8.0,
     'relb_table': 7.696,
     'ln2_g': 2.881,
     'ln2_b': 2.837,
     't5_table': 3.748}
    for name, (base, spread) in spreads.items():
        noise = np.random.default_rng([zlib.crc32(name.encode()), seed]).standard_normal(out[name].shape)
        drawn = base * np.exp(spread * noise) if base else spread * noise
        out[name] = __import__('jax').numpy.asarray(drawn.astype(out[name].dtype))
    for name, factor in factors.items():
        out[name] = (out[name] * factor).astype(out[name].dtype)
    return out
```

```python
from contextlib import ExitStack

import concourse.bass as bass
from concourse import mybir
import numpy as np

F32 = mybir.dt.float32
I32 = mybir.dt.int32
ALU = mybir.AluOpType
ACT = mybir.ActivationFunctionType
AX = mybir.AxisListType

P = 128
SEQ, D, FF, PLE = 256, 2048, 1024, 256
CHUNK, HD, HA, KVA, HB = 64, 64, 16, 2, 16
REL_CLIP, REL_TABLE = 256, 320
T5_BUCKETS, T5_MAX_DISTANCE = 32, 64
NE, NG, EPG = 16, 4, 4
ALPHA = 2.0 ** 0.25
LN_EPS = 1e-5
NEG = -1e30
SCALE = float(HD) ** -0.5

TT = SEQ // P
KT = D // P
PANEL = 512
NP_ = D // PANEL
VEC = 384

C_QA, C_KA, C_VA = 0, HA * HD, HA * HD + KVA * HD
C_QB = C_VA + KVA * HD
C_KB, C_VB = C_QB + HB * HD, C_QB + 2 * HB * HD
C_GA = C_QB + 3 * HB * HD
C_GB = C_GA + D

RING = 8
CW = 2048
N_KVA, N_Q, N_V, N_G, N_M, N_PLE, N_O, N_PG = 2, 24, 8, 32, 16, 2, 16, 16
K_KVA = 0
K_Q = K_KVA + N_KVA
K_V = K_Q + N_Q
K_G = K_V + N_V
K_M = K_G + N_G
K_PLE = K_M + N_M
K_O = K_PLE + N_PLE
K_PG = K_O + N_O
K_MOE = K_PG + N_PG
W1C = 8
PAIR = 2 * 3 * W1C
assert N_Q % RING == N_M % RING == N_O % RING == N_PG % RING == PAIR % RING == 0

SLOTS = 64
NPAIR = NE // 2
MAXPASS = SEQ // SLOTS
ECOLS = MAXPASS * NE + 2

P_KVA, P_Q, P_V, P_G, P_M, P_PLE, P_O, P_PG = 1, 2, 8, 10, 18, 26, 30, 34


def t5_bucket(rel):
    nb = T5_BUCKETS // 2
    ret = (rel > 0).astype(np.int32) * nb
    n = np.abs(rel)
    max_exact = nb // 2
    large = max_exact + (np.log(np.maximum(n, 1).astype(np.float32) / max_exact)
                         / np.log(T5_MAX_DISTANCE / max_exact) * (nb - max_exact)).astype(np.int32)
    return ret + np.where(n < max_exact, n, np.minimum(large, nb - 1))


def shape_constants():
    k = np.arange(P)
    square = np.zeros((P, 3 * P + SLOTS), np.float32)
    square[:, 0:P] = np.eye(P)
    square[:, P:2 * P] = k[:, None] < k[None, :]
    square[:, 2 * P:3 * P] = np.eye(P)[:, ::-1]
    square[:, 3 * P:] = np.arange(SLOTS)[None, :]
    bucket = (np.arange(T5_BUCKETS)[:, None] == t5_bucket(np.arange(VEC)[::-1] - REL_CLIP)[None, :]).astype(np.float32)
    return square, bucket


def build(nc, x, p, w_in, w_pa, w_pb, w_o, attn_sinks, relb_table, ln1_g, ln1_b, w_router, b_router,
          w1, w3, w2, w_ple, w_ple_gate, ln2_g, ln2_b, t5_table, square, bucket, out):
    with ExitStack() as ctx:
        def sb(name, shape, dt=F32):
            return ctx.enter_context(nc.sbuf_tensor(name, shape, dt))

        def sem(name):
            return ctx.enter_context(nc.semaphore(name))

        ring = sb("ring", [P, RING, CW])
        X = sb("X", [P, TT, D])
        XT = sb("XT", [P, KT, SEQ])
        bias = sb("bias", [P, HA + HB, SEQ])
        QKT = sb("QKT", [P, 24, SEQ])
        KA = sb("KA", [P, KVA, SEQ])
        VA = sb("VA", [P, TT, KVA * HD])
        VB = sb("VB", [P, TT, HB * HD])
        gates = sb("gates", [P, 2, KT, SEQ])
        S = sb("S", [P, 2, 2, SEQ])
        PT = sb("PT", [P, 2, 4, P])
        WR = sb("WR", [P, KT, NE])
        ident = sb("ident", [P, P])
        tri = sb("tri", [P, P])
        slots = sb("slots", [P, SLOTS])
        nsink = sb("nsink", [P, HA])
        sink = sb("sink", [P, HA])
        brt = sb("brt", [P, NE])
        posm = sb("posm", [P, TT, ECOLS])
        wsel = sb("wsel", [P, TT, ECOLS])
        nmax = sb("nmax", [P, 2, 2])
        esum = sb("esum", [P, 2, 2])
        esink = sb("esink", [P, 2, 2])
        rden = sb("rden", [P, 2, 2])
        stats = sb("stats", [P, TT, NP_, 6])
        mv = sb("mv", [P, TT, 2])
        rstd = sb("rstd", [P, TT])
        epst = sb("epst", [P, 1])
        n_it_t = sb("n_it_t", [1, 1], I32)
        acc = bias[:, 0:16, :].rearrange("q h k -> q (h k)").rearrange("q (t d) -> q t d", t=TT)
        buckets = S[0:T5_BUCKETS, 0, :, :].rearrange("q a b -> q (a b)")[:, 0:VEC]
        t5t = S[0:T5_BUCKETS, 1, 0, 0:HA]
        relt = PT[:, 0, 0, 0:3 * HB].rearrange("q (a h) -> q a h", a=3)
        flip = PT[:, 0, 1, :]
        vecA = PT[0:HA, 1, 0:3, :].rearrange("h a b -> h (a b)")
        vecB = gates[0:HB, 0, 0:2, :].rearrange("h a b -> h (a b)")[:, 0:VEC]
        pnat = S[:, 0, :, :]
        pT = PT[:, 0, :, :].rearrange("q (k t) c -> q k (t c)", k=2)
        g1 = VB[:, :, :].rearrange("q t d -> q (t d)")
        b1 = QKT[:, 16:24, :].rearrange("q a b -> q (a b)")
        g2 = QKT[:, 0:8, :].rearrange("q a b -> q (a b)")
        b2 = QKT[:, 8:16, :].rearrange("q a b -> q (a b)")
        rt = gates[:, 1, 8, :]
        sig = gates[:, 1, 9:13, :].rearrange("q a b -> q (a b)").rearrange("q (t n) -> q t n", t=TT)
        YT = gates[:, 0, 0:8, :].rearrange("q a b -> q (a b)").rearrange("q (d s) -> q d s", d=KT)
        XG = gates[:, 0, 8:12, :].rearrange("q a b -> q (a b)").rearrange("q (d s) -> q d s", d=KT)
        HS = gates[:, 0, 12:14, :].rearrange("q a b -> q (a b)")
        HT = gates[:, 0, 14:16, :].rearrange("q a b -> q (a b)").rearrange("q (f s) -> q f s", f=8)
        YN = gates[:, 1, 0:2, :].rearrange("q a b -> q (a b)")
        CT = gates[:, 1, 2, :]
        OH = gates[:, 1, 3, :].rearrange("q (e t s) -> q e t s", e=2, t=TT)
        OHW = gates[:, 1, 4, :].rearrange("q (t e s) -> q t e s", t=TT, e=2)
        ones = gates[:, 1, 5, 0:P]

        r_ex, r_pr = rt[:, 0:32], rt[:, 32:64]
        r_sel, r_rank = rt[:, 64:96], rt[:, 96:128]
        r_g, r_mask = rt[:, 128:160], rt[:, 160:192]
        r_gs, r_gr = rt[:, 192:200], rt[:, 200:208]
        r_gg, r_gm = rt[:, 208:216], rt[:, 216:224]
        r_m, r_s, r_w = rt[:, 224:226], rt[:, 226:228], rt[:, 228:230]
        r_c, r_c3 = rt[:, 230:231], rt[:, 231:234]

        PS = ctx.enter_context(nc.psum_tensor("PS", [P, 8, 512], F32))
        B_LOGIT, B_PT, B_Y = 4, 6, 7
        B_G, B_H1, B_H3, B_YT, B_T, B_S = 0, 2, 3, 4, 6, 7

        scratch = nc.dram_tensor("bias_vectors", [HA + HB, VEC], F32, kind="Internal").ap()

        weights_in = [sem(f"weights_in{s}") for s in range(RING)]
        weights_used = sem("weights_used")
        x_in = sem("x_in")
        const_in = sem("const_in")
        table_in = sem("table_in")
        small_in = sem("small_in")
        vec_ready = sem("vec_ready")
        vec_out = sem("vec_out")
        bias_in = sem("bias_in")
        bias_masked = sem("bias_masked")
        sink_ready = sem("sink_ready")
        vec_ps = sem("vec_ps")
        xt_ps = sem("xt_ps")
        xt_act, xt_dve = sem("xt_act"), sem("xt_dve")
        ev_act, ev_dve = sem("ev_act"), sem("ev_dve")
        logits_ps = sem("logits_ps")
        dve_step = sem("dve_step")
        max_ready, exp_ready, rden_ready, probs_ready = sem("max_ready"), sem("exp_ready"), sem("rden_ready"), sem("probs_ready")
        pt_ps, pt_ready, y_ps, y_ready = sem("pt_ps"), sem("pt_ready"), sem("y_ps"), sem("y_ready")
        gate_sig, merged = sem("gate_sig"), sem("merged")
        p_in, p_ps, p_ready = sem("p_in"), sem("p_ps"), sem("p_ready")
        ln_in = sem("ln_in")
        ln2_in = sem("ln2_in")
        var_ready, std_ready, norm_ready = sem("var_ready"), sem("std_ready"), sem("norm_ready")
        gain_ready = sem("gain_ready")
        x1_ready = sem("x1_ready")
        router_ps, rmax_ready, rexp_ready, mask_ready, pos_ps, routed = (
            sem("router_ps"), sem("rmax_ready"), sem("rexp_ready"), sem("mask_ready"), sem("pos_ps"), sem("routed"))
        sig_ready, acc_written = sem("sig_ready"), sem("acc_written")
        onehot_ready, gathered, xg_act, xg_dve = sem("onehot_ready"), sem("gathered"), sem("xg_act"), sem("xg_dve")
        silu_ready, h_ready, yt_act, yt_dve = sem("silu_ready"), sem("h_ready"), sem("yt_act"), sem("yt_dve")
        spread_ready, ct_ps, ct_ready = sem("spread_ready"), sem("ct_ps"), sem("ct_ready")
        yn_ps, yn_ready, sum_ps = sem("yn_ps"), sem("yn_ready"), sem("sum_ps")
        out_ready, out_done = sem("out_ready"), sem("out_done")

        block = ctx.enter_context(nc.Block())

        def slot(k):
            return ring[:, k % RING, :]

        def slot_kn(k, n):
            return slot(k).rearrange("q (k n) -> q k n", n=n)

        @block.sync
        def _(sp):
            def load(k, src, width):
                if k >= RING:
                    sp.wait_ge(weights_used, k - RING + 1)
                sp.dma_start(slot_kn(k, width), src).then_inc(weights_in[k % RING], 16)

            def rows(w, k0, nk, c0, width):
                return w[k0 * P:(k0 + nk) * P, c0:c0 + width].rearrange("(k p) n -> p k n", p=P)

            for c in range(N_KVA):
                load(K_KVA + c, rows(w_in[0], 8 * c, 8, C_KA, 2 * KVA * HD), 2 * KVA * HD)
            k = K_Q
            for c0 in (C_QA, C_QA + PANEL, C_QB, C_QB + PANEL, C_KB, C_KB + PANEL, C_VB, C_VB + PANEL,
                       *(C_GA + PANEL * j for j in range(2 * NP_))):
                for q in range(4):
                    load(k, rows(w_in[0], 4 * q, 4, c0, PANEL), PANEL)
                    k += 1
            for j in range(NP_):
                for w in (w_pa, w_pb):
                    for q in range(2):
                        load(k, rows(w[0], 4 * q, 4, PANEL * j, PANEL), PANEL)
                        k += 1
            for c in range(N_PLE):
                load(k, rows(w_ple[0], 0, 2, 1024 * c, 1024), 1024)
                k += 1
            for w in (w_o, w_ple_gate):
                for j in range(NP_):
                    for q in range(4):
                        load(k, rows(w[0], 4 * q, 4, PANEL * j, PANEL), PANEL)
                        k += 1
            assert k == K_MOE

            def pair_loads(pair, it):
                for c in range(PAIR):
                    e, m, q = c // (3 * W1C), c // W1C % 3, c % W1C
                    expert = bass.ds(pair * 2 + e, 1)
                    if m < 2:
                        src = (w1, w3)[m][0][expert, 2 * P * q:2 * P * (q + 1), :].rearrange("e (k p) n -> p (e k) n", p=P)
                        dst = slot_kn(K_MOE + c, FF)
                    else:
                        src = w2[0][expert, P * q:P * (q + 1), :].rearrange("e (k p) n -> p (e k) n", p=P)
                        dst = slot_kn(K_MOE + c, D)
                    sp.wait_ge(weights_used, it * PAIR + (K_MOE + c - RING + 1))
                    sp.dma_start(dst, src).then_inc(weights_in[(K_MOE + c) % RING], 16)

            with sp.Fori(0, NPAIR) as pair:
                pair_loads(pair, pair)
            sp.wait_ge(routed, 1)
            n_it = sp.value_load(n_it_t[0:1, 0:1], min_val=NPAIR, max_val=NPAIR * MAXPASS)
            with sp.If(n_it > NPAIR):
                with sp.Fori(NPAIR, n_it, NPAIR) as first:
                    with sp.Fori(0, NPAIR) as pair:
                        pair_loads(pair, first + pair)

        @block.gpsimd
        def _(pool):
            for s in range(32):
                kt = s % 2 + 1
                pool.wait_ge(rden_ready, s + 1)
                for sub in range(2):
                    last = pool.tensor_scalar(S[:, s % 2, sub, 0:kt * P], S[:, s % 2, sub, 0:kt * P],
                                              rden[:, s % 2, sub:sub + 1], None, ALU.mult)
                last.then_inc(probs_ready, 1)

        @block.scalar
        def _(act):
            for t in range(TT):
                act.dma_start(X[:, t, :], x[0, t * P:(t + 1) * P, :]).then_inc(x_in, 16)
            act.dma_start(ident[:, :], square[:, 0:P]).then_inc(const_in, 16)
            act.dma_start(tri[:, :], square[:, P:2 * P]).then_inc(const_in, 16)
            act.dma_start(slots[:, :], square[:, 3 * P:]).then_inc(const_in, 16)
            act.dma_start(flip, square[:, 2 * P:3 * P]).then_inc(const_in, 16)
            act.dma_start(buckets, bucket[:, :]).then_inc(table_in, 16)
            act.dma_start(t5t, t5_table[:, :]).then_inc(table_in, 16)
            act.dma_start(relt[:, 0:2, :], relb_table[0, 0:2 * P, :].rearrange("(a p) h -> p a h", p=P)).then_inc(table_in, 16)
            act.dma_start(relt[0:REL_TABLE - 2 * P, 2, :], relb_table[0, 2 * P:REL_TABLE, :]).then_inc(table_in, 16)
            act.dma_start(sink[:, :], attn_sinks.partition_broadcast(P).rearrange("p a h -> p (a h)")).then_inc(small_in, 16)
            act.dma_start(brt[:, :], b_router.partition_broadcast(P)).then_inc(small_in, 16)
            act.dma_start(WR[:, :, :], w_router.rearrange("(k p) e -> p k e", p=P)).then_inc(small_in, 16)

            for g in range(0, 8, 2):
                act.wait_ge(xt_ps, g + 1)
                act.copy(XT[:, 2 * g:2 * g + 2, :].rearrange("q a b -> q (a b)"), PS[:, g, :]).then_inc(xt_act, 1)

            act.wait_ge(vec_ready, 2)
            act.dma_start(scratch[0:HA, :], vecA).then_inc(vec_out, 16)
            act.dma_start(scratch[HA:HA + HB, :], vecB).then_inc(vec_out, 16)
            act.wait_ge(vec_out, 32)
            for g in range(4):
                band = bass.AP(tensor=scratch.tensor, offset=8 * g * VEC, ap=[[1, P], [VEC, 8], [1, SEQ]])
                act.dma_start(bias[:, 8 * g:8 * g + 8, :], band).then_inc(bias_in, 16)

            act.wait_ge(weights_used, K_Q)
            for kv in range(KVA):
                for half in range(2):
                    last = act.copy(KA[HD * half:HD * half + HD, kv, :], PS[HD * kv:HD * kv + HD, 2 * P_KVA, 0:SEQ])
                last.then_inc(ev_act, 1)

            with act.Fori(0, N_Q // RING) as body:
                for j in range(2):
                    act.wait_ge(weights_used, body * RING + (K_Q + 4 * j + 4))
                    act.copy(QKT[:, bass.ds(body * 8 + 4 * j, 2), :].rearrange("q a b -> q (a b)"),
                             PS[:, 2 * ((P_Q + j) % 2), :]).then_inc(ev_act, 1)
            for j in range(2):
                act.wait_ge(weights_used, K_V + 4 * j + 4)
                act.copy(VB[:, 0, PANEL * j:PANEL * (j + 1)], PS[:, 2 * ((P_V + j) % 2), :]).then_inc(ev_act, 1)

            def exps(s):
                act.wait_ge(max_ready, s + 1)
                kt = s % 2 + 1
                for sub in range(2):
                    last = act.activation(S[:, s % 2, sub, 0:kt * P], S[:, s % 2, sub, 0:kt * P], ACT.Exp,
                                          bias=nmax[:, s % 2, sub:sub + 1], accum_out=esum[:, s % 2, sub:sub + 1])
                if s < 16:
                    last = act.activation(esink[:, s % 2, :], esink[:, s % 2, :], ACT.Exp)
                last.then_inc(exp_ready, 1)

            def pt_copy(s):
                act.wait_ge(pt_ps, s + 1)
                kt = s % 2 + 1
                act.copy(PT[:, s % 2, 0:2 * kt, :].rearrange("q a b -> q (a b)"),
                         PS[:, B_PT, 0:2 * kt * P]).then_inc(pt_ready, 1)

            for s in range(33):
                if s >= 1:
                    pt_copy(s - 1)
                if s < 32:
                    exps(s)
                if s % 4 == 3:
                    j = s // 4
                    act.wait_ge(weights_used, K_G + 4 * j + 4)
                    act.copy(gates[:, j // 4, 4 * (j % 4):4 * (j % 4) + 2, :].rearrange("q a b -> q (a b)"),
                             PS[:, 2 * ((P_G + j) % 2), :]).then_inc(ev_act, 1)
            act.wait_ge(y_ready, 32)
            act.dma_start(g1, ln1_g.partition_broadcast(P).rearrange("p a d -> p (a d)")).then_inc(ln_in, 16)
            act.dma_start(b1, ln1_b.partition_broadcast(P).rearrange("p a d -> p (a d)")).then_inc(ln_in, 16)
            act.dma_start(pnat, p[0, 0].rearrange("(t q) c -> q t c", q=P)).then_inc(p_in, 16)

            act.wait_ge(ev_dve, P_M)
            act.wait_ge(ev_act, P_M)
            for j in range(NP_):
                for br in range(2):
                    g = gates[:, br, 4 * j:4 * j + 4, :].rearrange("q a b -> q (a b)")
                    act.activation(g, g, ACT.Sigmoid).then_inc(gate_sig, 1)
            act.wait_ge(p_ps, 1)
            act.copy(pT.rearrange("q k t -> q (k t)"), PS[:, B_PT, :]).then_inc(p_ready, 1)
            act.wait_ge(weights_used, K_PLE)
            act.dma_start(g2, ln2_g.partition_broadcast(P).rearrange("p a d -> p (a d)")).then_inc(ln2_in, 16)
            act.dma_start(b2, ln2_b.partition_broadcast(P).rearrange("p a d -> p (a d)")).then_inc(ln2_in, 16)

            def layer_norm(r, n):
                act.wait_ge(var_ready, n)
                act.activation(rstd[:, :], mv[:, :, 1], ACT.Sqrt, bias=epst[:, 0:1]).then_inc(std_ready, 1)

            layer_norm(X, 1)

            for g in range(0, 8, 2):
                act.wait_ge(xt_ps, 8 + g + 1)
                act.copy(XT[:, 2 * g:2 * g + 2, :].rearrange("q a b -> q (a b)"), PS[:, g, :]).then_inc(xt_act, 1)

            act.wait_ge(rmax_ready, 1)
            for t in range(TT):
                last = act.activation(r_ex[:, NE * t:NE * t + NE], PS[:, B_LOGIT, NE * t:NE * t + NE], ACT.Exp,
                                      bias=r_m[:, t:t + 1], accum_out=r_s[:, t:t + 1])
            last.then_inc(rexp_ready, 1)

            for j in range(NP_):
                act.wait_ge(weights_used, K_PG + 4 * j + 4)
                if j >= 1:
                    act.wait_ge(acc_written, j)
                act.activation(sig, PS[:, 2 * ((P_PG + j) % 2):2 * ((P_PG + j) % 2) + 2, :], ACT.Sigmoid).then_inc(sig_ready, 1)

            act.wait_ge(routed, 1)
            n_it = act.value_load(n_it_t[0:1, 0:1], min_val=NPAIR, max_val=NPAIR * MAXPASS)

            def yn_copy(it, j):
                act.wait_ge(yn_ps, it * 4 + (j + 1))
                act.copy(YN, PS[:, B_T, :]).then_inc(yn_ready, 1)

            def ct_copy(it):
                act.wait_ge(ct_ps, it + 1)
                act.copy(CT, PS[:, B_T, 0:SEQ]).then_inc(ct_ready, 1)

            with act.Fori(0, n_it) as it:
                for e in range(2):
                    act.wait_ge(gathered, it * 2 + (e + 1))
                    act.copy(XG[:, 0:8, :].rearrange("q d s -> q (d s)"), PS[:, B_G, :]).then_inc(xg_act, 1)
                    if e == 0:
                        ct_copy(it)
                        yn_copy(it, 0)
                        yn_copy(it, 1)
                    else:
                        act.wait_ge(weights_used, it * PAIR + (K_MOE + 24))
                        act.copy(YT[:, 0:8, 0:SLOTS], PS[:, B_YT, :].rearrange("q (d s) -> q d s", s=SLOTS)).then_inc(yt_act, 1)
                    act.wait_ge(weights_used, it * PAIR + (K_MOE + 24 * e + 8))
                    act.activation(HS, PS[:, B_H1, :], ACT.Silu).then_inc(silu_ready, 1)
                    if e == 0:
                        yn_copy(it, 2)
                        yn_copy(it, 3)
                act.wait_ge(weights_used, it * PAIR + (K_MOE + 48))
                act.copy(YT[:, 0:8, SLOTS:2 * SLOTS], PS[:, B_YT, :].rearrange("q (d s) -> q d s", s=SLOTS)).then_inc(yt_act, 1)
            ct_copy(n_it)
            for j in range(NP_):
                yn_copy(n_it, j)

            layer_norm(acc, 2)
            for t in range(TT):
                act.wait_ge(out_ready, t + 1)
                act.dma_start(out[0, t * P:(t + 1) * P, :], acc[:, t, :]).then_inc(out_done, 16)
            act.wait_ge(out_done, 16 * TT)

        @block.tensor
        def _(pe):
            def arrived(k, more=0):
                pe.wait_ge(weights_in[k % RING], more * 16 + 16 * (k // RING + 1))

            def bank_pair(n):
                return PS[:, 2 * (n % 2):2 * (n % 2) + 2, :]

            def columns(k, ps, rhs, first, last, w=PANEL):
                n = CW // w
                o = ps.rearrange("q a (b t) -> q (a b) t", t=SEQ)
                for q in range(n):
                    for m in range(4):
                        mm = pe.matmul(o[:, m, :], slot_kn(k, w)[:, q, P * m:P * m + P], rhs(q),
                                       start=(first and q == 0 and m % 2 == 0), stop=(last and q == n - 1),
                                       skip_group_check=True)
                mm.then_inc(weights_used, 1)

            def tokens(k, ps, lhs, first, last):
                for q in range(4):
                    for t in range(TT):
                        mm = pe.matmul(ps[:, t, :], lhs(q, t), slot_kn(k, PANEL)[:, q, :],
                                       start=(first and q == 0), stop=(last and q == 3), skip_group_check=True)
                mm.then_inc(weights_used, 1)

            def transpose_x(done):
                for g in range(8):
                    for b in range(4):
                        k, t = 2 * g + b // 2, b % 2
                        mm = pe.transpose(PS[:, g, P * b:P * b + P], X[:, t, P * k:P * k + P], ident[:, :])
                    mm.then_inc(xt_ps, 1)

            pe.wait_ge(x_in, 16 * TT)
            pe.wait_ge(const_in, 64)
            transpose_x(0)
            pe.wait_ge(xt_act, 4)
            pe.wait_ge(xt_dve, 4)
            pe.wait_ge(table_in, 64)
            pe.matmul(PS[0:HA, B_LOGIT, 0:VEC], t5t, buckets, start=True, stop=True)
            for a in range(3):
                n = min(P, REL_TABLE - P * a)
                mm = pe.matmul(PS[0:HB, B_LOGIT + 1, P * (3 - a) - n:P * (3 - a)], relt[0:n, a, :], flip[0:n, P - n:P],
                               start=True, stop=True)
            mm.then_inc(vec_ps, 1)

            for c in range(N_KVA):
                arrived(K_KVA + c)
                w = slot_kn(K_KVA + c, 2 * KVA * HD)
                for q in range(8):
                    k = 8 * c + q
                    pe.matmul(PS[:, 2 * P_KVA, 0:SEQ], w[:, q, 0:P], XT[:, k, :], start=(k == 0), stop=(k == KT - 1))
                    for t in range(TT):
                        mm = pe.matmul(PS[:, 2 * P_KVA + 1, P * t:P * t + P], XT[:, k, P * t:P * t + P], w[:, q, P:2 * P],
                                       start=(k == 0 and t == 0), stop=(k == KT - 1), skip_group_check=True)
                mm.then_inc(weights_used, 1)

            with pe.Fori(0, N_Q // RING) as body:
                for j in range(2):
                    pe.wait_ge(ev_act, body * 2 + (P_Q + j - 1))
                    pe.wait_ge(ev_dve, body * 2 + (P_Q + j - 1))
                    for c in range(4):
                        k = K_Q + 4 * j + c
                        arrived(k, body)
                        columns(k, bank_pair(P_Q + j), lambda q, c=c: XT[:, 4 * c + q, :], c == 0, c == 3)
            for j in range(2):
                pe.wait_ge(ev_act, P_V + j - 1)
                pe.wait_ge(ev_dve, P_V + j - 1)
                for c in range(4):
                    k = K_V + 4 * j + c
                    arrived(k)
                    tokens(k, bank_pair(P_V + j), lambda q, t, c=c: XT[:, 4 * c + q, P * t:P * t + P], c == 0, c == 3)

            def logits(s):
                br, i, t = s // 16, s % 16 // 2, s % 2
                keys = P * (t + 1)
                pe.wait_ge(max_ready, s)
                for sub in range(2):
                    h = slice(HD * sub, HD * sub + HD)
                    rhs = KA[h, i // 4, 0:keys] if br == 0 else QKT[h, 16 + i, 0:keys]
                    mm = pe.matmul(PS[:, B_LOGIT + sub, 0:keys], QKT[h, 8 * br + i, P * t:P * t + P],
                                   rhs, start=True, stop=True)
                mm.then_inc(logits_ps, 1)

            def transposes(s):
                t = s % 2
                pe.wait_ge(probs_ready, s + 1)
                pe.wait_ge(pt_ready, s)
                for sub in range(2):
                    for k in range(t + 1):
                        n = sub * (t + 1) + k
                        mm = pe.transpose(PS[:, B_PT, P * n:P * n + P], S[:, s % 2, sub, P * k:P * k + P], ident[:, :])
                mm.then_inc(pt_ps, 1)

            def values(s):
                br, i, t = s // 16, s % 16 // 2, s % 2
                pe.wait_ge(pt_ready, s + 1)
                pe.wait_ge(y_ready, s)
                for sub in range(2):
                    for k in range(t + 1):
                        v = VA[:, k, HD * (i // 4):HD * (i // 4) + HD] if br == 0 else VB[:, k, HD * (2 * i + sub):HD * (2 * i + sub + 1)]
                        mm = pe.matmul(PS[0:HD, B_Y, P * sub:P * sub + P], v, PT[:, s % 2, sub * (t + 1) + k, :],
                                       start=(k == 0), stop=(k == t))
                mm.then_inc(y_ps, 1)

            pe.wait_ge(bias_masked, 1)
            pe.wait_ge(ev_act, P_G - 1)
            pe.wait_ge(ev_dve, P_G - 1)
            for s in range(34):
                if s == 1:
                    pe.wait_ge(ev_act, P_G)
                    pe.wait_ge(ev_dve, P_G)
                if s < 32:
                    logits(s)
                if 1 <= s <= 32:
                    transposes(s - 1)
                if 2 <= s:
                    values(s - 2)
                if s < 32:
                    j, c = s // 4, s % 4
                    if c == 0:
                        pe.wait_ge(ev_act, P_G + j - 1)
                        pe.wait_ge(ev_dve, P_G + j - 1)
                    arrived(K_G + s)
                    columns(K_G + s, bank_pair(P_G + j), lambda q, c=c: XT[:, 4 * c + q, :], c == 0, c == 3)

            pe.wait_ge(y_ready, 32)
            pe.wait_ge(ev_act, P_M)
            with pe.Fori(0, N_M // RING) as body:
                for n in range(4):
                    pe.wait_ge(ev_dve, body * 4 + (P_M + n - 1))
                    for c in range(2):
                        k = K_M + 2 * n + c
                        arrived(k, body)
                        columns(k, bank_pair(P_M + n), lambda q, c=c, n=n: QKT[:, 8 * (n % 2) + 4 * c + q, :], c == 0, c == 1)

            pe.wait_ge(p_in, 16)
            for k in range(2):
                for t in range(TT):
                    mm = pe.transpose(PS[:, B_PT, P * (2 * k + t):P * (2 * k + t) + P], pnat[:, t, P * k:P * k + P], ident[:, :])
            mm.then_inc(p_ps, 1)
            pe.wait_ge(p_ready, 1)
            for c in range(N_PLE):
                k = K_PLE + c
                arrived(k)
                for j in range(2):
                    n = P_PLE + 2 * c + j
                    pe.wait_ge(ev_dve, n - 1)
                    for q in range(2):
                        for t in range(TT):
                            mm = pe.matmul(bank_pair(n)[:, t, :], pT[:, q, P * t:P * t + P],
                                           slot_kn(k, 1024)[:, q, PANEL * j:PANEL * j + PANEL], start=(q == 0), stop=(q == 1))
                mm.then_inc(weights_used, 1)

            pe.wait_ge(merged, NP_)
            with pe.Fori(0, N_O // RING) as body:
                for j in range(2):
                    pe.wait_ge(ev_dve, body * 2 + (P_O + j - 1))
                    for c in range(4):
                        k = K_O + 4 * j + c
                        arrived(k, body)
                        tokens(k, bank_pair(P_O + j), lambda q, t, c=c: gates[:, 0, 4 * c + q, P * t:P * t + P], c == 0, c == 3)

            pe.wait_ge(x1_ready, 1)
            transpose_x(1)
            pe.wait_ge(xt_act, 8)
            pe.wait_ge(xt_dve, 8)
            pe.wait_ge(small_in, 48)
            for t in range(TT):
                for k in range(KT):
                    mm = pe.matmul(PS[:, B_LOGIT, NE * t:NE * t + NE], XT[:, k, P * t:P * t + P], WR[:, k, :],
                                   start=(k == 0), stop=(k == KT - 1))
            mm.then_inc(router_ps, 1)

            def positions():
                pe.wait_ge(mask_ready, 1)
                m = r_mask.rearrange("q (t e) -> q t e", t=TT)
                o = PS[:, B_LOGIT + 1, 0:3 * NE].rearrange("q (t e) -> q t e", e=NE)
                pe.matmul(o[:, 0, :], tri[:, :], m[:, 0, :], start=True, stop=True)
                pe.matmul(o[:, 1, :], ones, m[:, 0, :], start=True, stop=False)
                pe.matmul(o[:, 1, :], tri[:, :], m[:, 1, :], start=False, stop=True)
                pe.matmul(o[:, 2, :], ones, m[:, 0, :], start=True, stop=False)
                pe.matmul(o[:, 2, :], ones, m[:, 1, :], start=False, stop=True).then_inc(pos_ps, 1)

            for j in range(NP_):
                if j == 1:
                    positions()
                if j >= 2:
                    pe.wait_ge(sig_ready, j - 1)
                for c in range(4):
                    k = K_PG + 4 * j + c
                    arrived(k)
                    tokens(k, bank_pair(P_PG + j), lambda q, t, c=c: XT[:, 4 * c + q, P * t:P * t + P], c == 0, c == 3)

            pe.wait_ge(routed, 1)
            n_it = pe.value_load(n_it_t[0:1, 0:1], min_val=NPAIR, max_val=NPAIR * MAXPASS)
            pe.wait_ge(sig_ready, NP_)

            def gather(it, e):
                pe.wait_ge(onehot_ready, it * 2 + (e + 1))
                o = PS[:, B_G:B_G + 2, :].rearrange("q a (d s) -> q (a d) s", s=SLOTS)
                for d in range(KT):
                    for t in range(TT):
                        mm = pe.matmul(o[:, d, :], X[:, t, P * d:P * d + P], OH[:, e, t, :],
                                       start=(d % 8 == 0 and t == 0), stop=(t == TT - 1), skip_group_check=True)
                mm.then_inc(gathered, 1)

            def up(it, e, m, c):
                k = K_MOE + 24 * e + 8 * m + c
                arrived(k, it * (PAIR // RING))
                o = PS[:, B_H1 + m, :].rearrange("q (f s) -> q f s", s=SLOTS)
                for q in range(2):
                    for f in range(FF // P):
                        mm = pe.matmul(o[:, f, :], slot_kn(k, FF)[:, q, P * f:P * f + P], XG[:, 2 * c + q, :],
                                       start=(c == 0 and q == 0 and f == 0), stop=(c == 7 and q == 1), skip_group_check=True)
                mm.then_inc(weights_used, 1)

            def down(it, e, c):
                k = K_MOE + 24 * e + 16 + c
                arrived(k, it * (PAIR // RING))
                o = PS[:, B_YT:B_YT + 2, :].rearrange("q a (d s) -> q (a d) s", s=SLOTS)
                for d in range(KT):
                    mm = pe.matmul(o[:, d, :], slot(k)[:, P * d:P * d + P], HT[:, c, :],
                                   start=(c == 0 and d % 8 == 0), stop=(c == 7), skip_group_check=True)
                mm.then_inc(weights_used, 1)

            def spread_matrix(it):
                pe.wait_ge(spread_ready, it + 1)
                for t in range(TT):
                    mm = pe.transpose(PS[:, B_T, P * t:P * t + P], OHW[:, t, :, :].rearrange("q e s -> q (e s)"), ident[:, :])
                mm.then_inc(ct_ps, 1)

            def turn(it, j):
                pe.wait_ge(ct_ready, it + 1)
                pe.wait_ge(yt_act, it * 2 + 1)
                pe.wait_ge(yt_dve, it * 2 + 1)
                for b in range(4):
                    mm = pe.transpose(PS[:, B_T, P * b:P * b + P], YT[:, 4 * j + b, :], ident[:, :])
                mm.then_inc(yn_ps, 1)

            def spread(it, j, t):
                pe.wait_ge(yn_ready, it * 4 + (j + 1))
                pe.wait_ge(acc_written, it * 8 + (NP_ + 2 * j + t))
                pe.matmul(PS[:, B_S, :], CT[:, P * t:P * t + P], YN, start=True, stop=True).then_inc(sum_ps, 1)

            def spread_step(it, n):
                if n == 0:
                    spread_matrix(it)
                elif n <= 12:
                    j, a = (n - 1) // 3, (n - 1) % 3
                    if a == 0:
                        turn(it, j)
                    else:
                        spread(it, j, a - 1)

            with pe.Fori(0, n_it) as it:
                for e in range(2):
                    if e == 0:
                        gather(it, 0)
                    pe.wait_ge(xg_act, it * 2 + (e + 1))
                    pe.wait_ge(xg_dve, it * 2 + (e + 1))
                    for m in range(2):
                        for c in range(W1C):
                            up(it, e, m, c)
                            if e == 0:
                                spread_step(it, 8 * m + c)
                    if e == 0:
                        gather(it, 1)
                    pe.wait_ge(h_ready, it * 2 + (e + 1))
                    pe.wait_ge(yt_act, it * 2 + (e + 1))
                    pe.wait_ge(yt_dve, it * 2 + (e + 1))
                    for c in range(W1C):
                        down(it, e, c)
            for n in range(13):
                spread_step(n_it, n)

        @block.vector
        def _(dve):
            steps = [0]

            def link(ins, base=0):
                steps[0] += 1
                ins.then_inc(dve_step, 1)
                dve.wait_ge(dve_step, base + steps[0])

            def bank2(n, b):
                return PS[:, 2 * (n % 2) + b, :]

            dve.memset(epst[:, :], LN_EPS)
            dve.memset(vecB[:, 0:VEC - REL_TABLE], 0.0)
            for g in range(1, 8, 2):
                dve.wait_ge(xt_ps, g + 1)
                dve.tensor_copy(XT[:, 2 * g:2 * g + 2, :].rearrange("q a b -> q (a b)"), PS[:, g, :]).then_inc(xt_dve, 1)
            dve.wait_ge(vec_ps, 1)
            dve.tensor_copy(vecA, PS[0:HA, B_LOGIT, 0:VEC]).then_inc(vec_ready, 1)
            dve.tensor_copy(vecB[:, VEC - REL_TABLE:VEC], PS[0:HB, B_LOGIT + 1, VEC - REL_TABLE:VEC]).then_inc(vec_ready, 1)
            dve.wait_ge(small_in, 48)
            dve.tensor_scalar(nsink[:, :], sink[:, :], -1.0, None, ALU.mult).then_inc(sink_ready, 1)

            dve.wait_ge(weights_used, K_Q)
            for t in range(TT):
                dve.tensor_copy(VA[:, t, :], PS[:, 2 * P_KVA + 1, P * t:P * t + P]).then_inc(ev_dve, 1)
            with dve.Fori(0, N_Q // RING) as body:
                for j in range(2):
                    dve.wait_ge(weights_used, body * RING + (K_Q + 4 * j + 4))
                    dve.tensor_copy(QKT[:, bass.ds(body * 8 + 4 * j + 2, 2), :].rearrange("q a b -> q (a b)"),
                                    bank2(P_Q + j, 1)).then_inc(ev_dve, 1)
            dve.wait_ge(bias_in, 64)
            dve.memset(bias[0:CHUNK, 0:HA, 3 * CHUNK:SEQ], NEG)
            dve.memset(bias[CHUNK:P, 0:HA, P:SEQ], NEG)
            dve.memset(bias[0:CHUNK, :, 0:CHUNK], NEG).then_inc(bias_masked, 1)
            for j in range(2):
                dve.wait_ge(weights_used, K_V + 4 * j + 4)
                dve.tensor_copy(VB[:, 1, PANEL * j:PANEL * (j + 1)], bank2(P_V + j, 1)).then_inc(ev_dve, 1)

            dve.wait_ge(bias_masked, 1)
            dve.wait_ge(sink_ready, 1)

            def biased(s):
                br, i, t = s // 16, s % 16 // 2, s % 2
                keys, b = P * (t + 1), s % 2
                dve.wait_ge(logits_ps, s + 1)
                if s >= 2:
                    dve.wait_ge(pt_ps, s - 1)
                ps = PS[:, B_LOGIT:B_LOGIT + 2, 0:keys]
                h0 = HA * br + 2 * i
                link(dve.scalar_tensor_tensor(out=S[:, b, :, 0:keys], in0=ps, scalar=SCALE,
                                              in1=bias[:, h0:h0 + 2, 0:keys][:, :, ::-1], op0=ALU.mult, op1=ALU.add))
                if br == 1:
                    dve.tensor_reduce(nmax[:, b, :], S[:, b, :, 0:keys], AX.X, ALU.max, negate=True).then_inc(max_ready, 1)
                else:
                    link(dve.tensor_reduce(nmax[:, b, :], S[:, b, :, 0:keys], AX.X, ALU.max, negate=True))
                    link(dve.tensor_tensor(nmax[:, b, :], nmax[:, b, :], nsink[:, 2 * i:2 * i + 2], ALU.min))
                    dve.tensor_tensor(esink[:, b, :], sink[:, 2 * i:2 * i + 2], nmax[:, b, :], ALU.add).then_inc(max_ready, 1)

            def denominators(s):
                b = s % 2
                dve.wait_ge(exp_ready, s + 1)
                if s < 16:
                    link(dve.tensor_tensor(esum[:, b, :], esum[:, b, :], esink[:, b, :], ALU.add))
                dve.reciprocal(rden[:, b, :], esum[:, b, :]).then_inc(rden_ready, 1)

            def outputs(s):
                br, i, t = s // 16, s % 16 // 2, s % 2
                dve.wait_ge(y_ps, s + 1)
                for sub in range(2):
                    last = dve.tensor_copy(QKT[HD * sub:HD * sub + HD, 8 * br + i, P * t:P * t + P],
                                           PS[0:HD, B_Y, P * sub:P * sub + P])
                last.then_inc(y_ready, 1)

            for s in range(34):
                if s < 32:
                    biased(s)
                    denominators(s)
                if s >= 2:
                    outputs(s - 2)
                if s < 32 and s % 4 == 3:
                    j = s // 4
                    dve.wait_ge(weights_used, K_G + 4 * j + 4)
                    dve.tensor_copy(gates[:, j // 4, 4 * (j % 4) + 2:4 * (j % 4) + 4, :].rearrange("q a b -> q (a b)"),
                                    bank2(P_G + j, 1)).then_inc(ev_dve, 1)

            for j in range(NP_):
                for br in range(2):
                    n = 2 * j + br
                    g = gates[:, br, 4 * j:4 * j + 4, :].rearrange("q a b -> q (a b)")
                    dve.wait_ge(gate_sig, n + 1)
                    dve.wait_ge(weights_used, K_M + 2 * n + 2)
                    ins = dve.tensor_tensor(g, PS[:, 2 * ((P_M + n) % 2):2 * ((P_M + n) % 2) + 2, :].rearrange("q a b -> q (a b)"), g, ALU.mult)
                    ins.then_inc(ev_dve, 1)
                dve.wait_ge(ev_dve, P_M + 2 * j + 2)
                ga = gates[:, 0, 4 * j:4 * j + 4, :].rearrange("q a b -> q (a b)")
                dve.tensor_tensor(ga, ga, g, ALU.add).then_inc(merged, 1)
            for n in range(NP_):
                dve.wait_ge(weights_used, K_PLE + n // 2 + 1)
                dve.tensor_copy(acc[:, :, PANEL * n:PANEL * n + PANEL],
                                PS[:, 2 * ((P_PLE + n) % 2):2 * ((P_PLE + n) % 2) + 2, :]).then_inc(ev_dve, 1)
            for j in range(NP_):
                dve.wait_ge(weights_used, K_O + 4 * j + 4)
                xs = X[:, :, PANEL * j:PANEL * j + PANEL]
                dve.scalar_tensor_tensor(out=xs, in0=xs, scalar=ALPHA,
                                         in1=PS[:, 2 * ((P_O + j) % 2):2 * ((P_O + j) % 2) + 2, :],
                                         op0=ALU.mult, op1=ALU.add).then_inc(ev_dve, 1)
                dve.wait_ge(ev_dve, P_O + j + 1)
                for t in range(TT):
                    last = dve.bn_stats(stats[:, t, j, :], X[:, t, PANEL * j:PANEL * j + PANEL])
            link(last)

            def normalise(r, n, g, b, done, vectors):
                for t in range(TT):
                    last = dve.bn_aggr(mv[:, t, :], stats[:, t, :, :].rearrange("q a b -> q (a b)"))
                last.then_inc(var_ready, 1)
                dve.wait_ge(std_ready, n)
                link(dve.reciprocal(rstd[:, :], rstd[:, :]))
                dve.wait_ge(vectors, 32)
                for t in range(TT):
                    link(dve.tensor_scalar(r[:, t, :], r[:, t, :], mv[:, t, 0:1], rstd[:, t:t + 1], ALU.subtract, ALU.mult))
                    link(dve.tensor_tensor(r[:, t, :], r[:, t, :], g, ALU.mult))
                    last = dve.tensor_tensor(r[:, t, :], r[:, t, :], b, ALU.add)
                    if done is out_ready:
                        last.then_inc(done, 1)
                if done is not out_ready:
                    last.then_inc(done, 1)

            normalise(X, 1, g1, b1, x1_ready, ln_in)

            dve.memset(ones, 1.0)
            dve.memset(OHW, 0.0).then_inc(spread_ready, 1)
            dve.memset(YT[:, 0:8, :], 0.0).then_inc(yt_act, 1)
            dve.memset(YT[:, 8:16, :], 0.0).then_inc(yt_dve, 1)
            for g in range(1, 8, 2):
                dve.wait_ge(xt_ps, 8 + g + 1)
                dve.tensor_copy(XT[:, 2 * g:2 * g + 2, :].rearrange("q a b -> q (a b)"), PS[:, g, :]).then_inc(xt_dve, 1)

            def te(a):
                return a.rearrange("q (t e) -> q t e", t=TT)

            def tge(a):
                return a.rearrange("q (t e) -> q t e", e=EPG)

            def rank(val, r, g, n):
                for i in range(n):
                    last = dve.memset(r[:, :, i], float(n - 1 - i))
                link(last)
                for s in range(1, n):
                    link(dve.tensor_tensor(g[:, :, 0:n - s], val[:, :, 0:n - s], val[:, :, s:n], ALU.is_ge))
                    link(dve.tensor_tensor(r[:, :, s:n], r[:, :, s:n], g[:, :, 0:n - s], ALU.add))
                    link(dve.tensor_tensor(r[:, :, 0:n - s], r[:, :, 0:n - s], g[:, :, 0:n - s], ALU.subtract))

            def route():
                lg = te(PS[:, B_LOGIT, 0:2 * NE])
                dve.wait_ge(router_ps, 1)
                dve.tensor_reduce(r_m, lg, AX.X, ALU.max, negate=True).then_inc(rmax_ready, 1)
                dve.wait_ge(rexp_ready, 1)
                link(dve.reciprocal(r_s, r_s))
                link(dve.tensor_tensor(te(r_pr), te(r_ex), r_s.unsqueeze(2).broadcast_to([P, TT, NE]), ALU.mult))
                link(dve.tensor_tensor(te(r_sel), te(r_pr), brt[:, :].unsqueeze(1).broadcast_to([P, TT, NE]), ALU.add))
                rank(tge(r_sel), tge(r_rank), tge(r_g), EPG)
                link(dve.tensor_scalar(r_rank, r_rank, 2.0, None, ALU.is_lt))
                link(dve.tensor_tensor(r_g, r_sel, r_rank, ALU.mult))
                link(dve.tensor_reduce(r_gs, tge(r_g), AX.X, ALU.add))
                rank(tge(r_gs), tge(r_gr), tge(r_gg), NG)
                link(dve.tensor_scalar(r_gm, r_gr, 1.0, None, ALU.is_lt))
                link(dve.tensor_tensor(tge(r_mask), tge(r_rank), r_gm.unsqueeze(2).broadcast_to([P, TT * NG, EPG]), ALU.mult))
                link(dve.tensor_tensor(r_g, r_pr, r_mask, ALU.mult))
                steps[0] += 1
                last = dve.tensor_reduce(r_w, te(r_g), AX.X, ALU.add)
                last.then_inc(dve_step, 1)
                dve.wait_ge(dve_step, steps[0])
                link(dve.reciprocal(r_w, r_w))
                dve.tensor_tensor(te(r_g), te(r_g), r_w.unsqueeze(2).broadcast_to([P, TT, NE]), ALU.mult).then_inc(mask_ready, 1)
                dve.wait_ge(mask_ready, 1)
                dve.memset(wsel[:, :, MAXPASS * NE:], 0.0)
                dve.memset(posm[:, :, MAXPASS * NE:], -1.0)
                for r in range(MAXPASS):
                    dve.tensor_copy(wsel[:, :, NE * r:NE * r + NE], te(r_g))
                dve.wait_ge(pos_ps, 1)
                pos = PS[:, B_LOGIT + 1, 0:3 * NE]
                link(dve.scalar_tensor_tensor(out=r_sel, in0=pos[:, 0:2 * NE], scalar=1.0, in1=r_mask, op0=ALU.add, op1=ALU.mult))
                for r in range(MAXPASS):
                    dve.tensor_scalar(posm[:, :, NE * r:NE * r + NE], te(r_sel), -1.0 - SLOTS * r, None, ALU.add)
                link(dve.tensor_reduce(r_c, pos[:, 2 * NE:3 * NE], AX.X, ALU.max))
                for r in range(1, MAXPASS):
                    link(dve.tensor_scalar(r_c3[:, r - 1:r], r_c, float(SLOTS * r), float(NPAIR), ALU.is_gt, ALU.mult))
                link(dve.tensor_reduce(r_c, r_c3, AX.X, ALU.add))
                dve.tensor_scalar(n_it_t[0:1, 0:1], r_c[0:1, :], float(NPAIR), None, ALU.add).then_inc(routed, 1)

            route()

            for j in range(NP_):
                dve.wait_ge(sig_ready, j + 1)
                a = acc[:, :, PANEL * j:PANEL * j + PANEL]
                link(dve.tensor_tensor(a, a, sig, ALU.mult))
                dve.scalar_tensor_tensor(out=a, in0=X[:, :, PANEL * j:PANEL * j + PANEL], scalar=ALPHA, in1=a,
                                         op0=ALU.mult, op1=ALU.add).then_inc(acc_written, 1)

            dve.wait_ge(routed, 1)
            n_it = dve.value_load(n_it_t[0:1, 0:1], min_val=NPAIR, max_val=NPAIR * MAXPASS)

            def onehots(it2):
                for e in range(2):
                    for t in range(TT):
                        last = dve.tensor_scalar(OH[:, e, t, :], slots[:, :], posm[:, t, bass.ds(it2 + e, 1)], None, ALU.is_equal)
                    last.then_inc(onehot_ready, 1)

            def spread_weights(it2):
                for e in range(2):
                    for t in range(TT):
                        last = dve.tensor_scalar(OHW[:, t, e, :], slots[:, :], posm[:, t, bass.ds(it2 + e, 1)],
                                                 wsel[:, t, bass.ds(it2 + e, 1)], ALU.is_equal, ALU.mult)
                last.then_inc(spread_ready, 1)

            def add_sum(it, n):
                j, t = n // 2, n % 2
                a = acc[:, t, PANEL * j:PANEL * j + PANEL]
                dve.wait_ge(sum_ps, it * 8 + (n + 1))
                dve.tensor_tensor(a, PS[:, B_S, :], a, ALU.add).then_inc(acc_written, 1)

            dve.wait_ge(acc_written, NP_)
            onehots(0)
            with dve.Fori(0, n_it) as it:
                for e in range(2):
                    dve.wait_ge(gathered, it * 2 + (e + 1))
                    dve.tensor_copy(XG[:, 8:16, :].rearrange("q d s -> q (d s)"), PS[:, B_G + 1, :]).then_inc(xg_dve, 1)
                    if e == 0:
                        for n in range(8):
                            add_sum(it, n)
                    else:
                        dve.wait_ge(weights_used, it * PAIR + (K_MOE + 24))
                        dve.tensor_copy(YT[:, 8:16, 0:SLOTS], PS[:, B_YT + 1, :].rearrange("q (d s) -> q d s", s=SLOTS)).then_inc(yt_dve, 1)
                    dve.wait_ge(weights_used, it * PAIR + (K_MOE + 24 * e + 16))
                    dve.wait_ge(silu_ready, it * 2 + (e + 1))
                    dve.tensor_tensor(HT.rearrange("q f s -> q (f s)"), PS[:, B_H3, :], HS, ALU.mult).then_inc(h_ready, 1)
                spread_weights(it * 2)
                onehots(it * 2 + 2)
                dve.wait_ge(weights_used, it * PAIR + (K_MOE + 48))
                dve.tensor_copy(YT[:, 8:16, SLOTS:2 * SLOTS], PS[:, B_YT + 1, :].rearrange("q (d s) -> q d s", s=SLOTS)).then_inc(yt_dve, 1)
            for n in range(8):
                add_sum(n_it, n)

            dve.wait_ge(acc_written, n_it * 8 + (NP_ + 8))
            for t in range(TT):
                for j in range(NP_):
                    last = dve.bn_stats(stats[:, t, j, :], acc[:, t, PANEL * j:PANEL * j + PANEL])
            link(last)
            normalise(acc, 2, g2, b2, out_ready, ln2_in)


_INS = ["x", "p", "w_in", "w_pa", "w_pb", "w_o", "attn_sinks", "relb_table", "ln1_g", "ln1_b", "w_router", "b_router",
        "w1", "w3", "w2", "w_ple", "w_ple_gate", "ln2_g", "ln2_b", "t5_table"]


def kernel(**inputs):
    import concourse.bacc as bacc
    from concourse.bass_utils import run_bass_kernel_spmd

    nc = bacc.Bacc("TRN2", target_bir_lowering=False, num_devices=1)
    arrays, args = {}, []
    square, bucket = shape_constants()
    for name, a in [(n, inputs[n]) for n in _INS] + [("square", square), ("bucket", bucket)]:
        a = np.ascontiguousarray(a)
        arrays[f"in_{name}"] = a
        args.append(nc.dram_tensor(f"in_{name}", a.shape, mybir.dt.from_np(a.dtype), kind="ExternalInput").ap())
    out = nc.dram_tensor("out", (1, SEQ, D), F32, kind="ExternalOutput").ap()
    build(nc, *args, out)
    r = run_bass_kernel_spmd(nc, [arrays], core_ids=[0])
    return r.results[0]["out"]
```

```python
from contextlib import ExitStack

import concourse.bass as bass
from concourse import mybir
import numpy as np

F32 = mybir.dt.float32
I32 = mybir.dt.int32
ALU = mybir.AluOpType
ACT = mybir.ActivationFunctionType
AX = mybir.AxisListType

P = 128
SEQ, D, FF, PLE = 256, 2048, 1024, 256
CHUNK, HD, HA, KVA, HB = 64, 64, 16, 2, 16
REL_CLIP, REL_TABLE = 256, 320
T5_BUCKETS, T5_MAX_DISTANCE = 32, 64
NE, NG, EPG = 16, 4, 4
ALPHA = 2.0 ** 0.25
LN_EPS = 1e-5
NEG = -1e30
SCALE = float(HD) ** -0.5

TT = SEQ // P
KT = D // P
PANEL = 512
NP_ = D // PANEL
VEC = 384

C_QA, C_KA, C_VA = 0, HA * HD, HA * HD + KVA * HD
C_QB = C_VA + KVA * HD
C_KB, C_VB = C_QB + HB * HD, C_QB + 2 * HB * HD
C_GA = C_QB + 3 * HB * HD
C_GB = C_GA + D

RING = 8
CW = 2048
N_KVA, N_Q, N_V, N_G, N_M, N_PLE, N_O, N_PG = 2, 24, 8, 32, 16, 2, 16, 16
K_KVA = 0
K_Q = K_KVA + N_KVA
K_V = K_Q + N_Q
K_G = K_V + N_V
K_M = K_G + N_G
K_PLE = K_M + N_M
K_O = K_PLE + N_PLE
K_PG = K_O + N_O
K_MOE = K_PG + N_PG
W1C = 8
PAIR = 2 * 3 * W1C
assert N_Q % RING == N_M % RING == N_O % RING == N_PG % RING == PAIR % RING == 0

SLOTS = 64
NPAIR = NE // 2
MAXPASS = SEQ // SLOTS
ECOLS = MAXPASS * NE + 2

P_KVA, P_Q, P_V, P_G, P_M, P_PLE, P_O, P_PG = 1, 2, 8, 10, 18, 26, 30, 34


def t5_bucket(rel):
    nb = T5_BUCKETS // 2
    ret = (rel > 0).astype(np.int32) * nb
    n = np.abs(rel)
    max_exact = nb // 2
    large = max_exact + (np.log(np.maximum(n, 1).astype(np.float32) / max_exact)
                         / np.log(T5_MAX_DISTANCE / max_exact) * (nb - max_exact)).astype(np.int32)
    return ret + np.where(n < max_exact, n, np.minimum(large, nb - 1))


def shape_constants():
    k = np.arange(P)
    square = np.zeros((P, 3 * P + SLOTS), np.float32)
    square[:, 0:P] = np.eye(P)
    square[:, P:2 * P] = k[:, None] < k[None, :]
    square[:, 2 * P:3 * P] = np.eye(P)[:, ::-1]
    square[:, 3 * P:] = np.arange(SLOTS)[None, :]
    bucket = (np.arange(T5_BUCKETS)[:, None] == t5_bucket(np.arange(VEC)[::-1] - REL_CLIP)[None, :]).astype(np.float32)
    return square, bucket


def build(nc, x, p, w_in, w_pa, w_pb, w_o, attn_sinks, relb_table, ln1_g, ln1_b, w_router, b_router,
          w1, w3, w2, w_ple, w_ple_gate, ln2_g, ln2_b, t5_table, square, bucket, out):
    with ExitStack() as ctx:
        def sb(name, shape, dt=F32):
            return ctx.enter_context(nc.sbuf_tensor(name, shape, dt))

        def sem(name):
            return ctx.enter_context(nc.semaphore(name))

        ring = sb("ring", [P, RING, CW])
        X = sb("X", [P, TT, D])
        XT = sb("XT", [P, KT, SEQ])
        bias = sb("bias", [P, HA + HB, SEQ])
        QKT = sb("QKT", [P, 24, SEQ])
        KA = sb("KA", [P, KVA, SEQ])
        VA = sb("VA", [P, TT, KVA * HD])
        VB = sb("VB", [P, TT, HB * HD])
        gates = sb("gates", [P, 2, KT, SEQ])
        S = sb("S", [P, 2, 2, SEQ])
        PT = sb("PT", [P, 2, 4, P])
        WR = sb("WR", [P, KT, NE])
        ident = sb("ident", [P, P])
        tri = sb("tri", [P, P])
        slots = sb("slots", [P, SLOTS])
        nsink = sb("nsink", [P, HA])
        sink = sb("sink", [P, HA])
        brt = sb("brt", [P, NE])
        posm = sb("posm", [P, TT, ECOLS])
        wsel = sb("wsel", [P, TT, ECOLS])
        nmax = sb("nmax", [P, 2, 2])
        esum = sb("esum", [P, 2, 2])
        esink = sb("esink", [P, 2, 2])
        rden = sb("rden", [P, 2, 2])
        stats = sb("stats", [P, TT, NP_, 6])
        mv = sb("mv", [P, TT, 2])
        rstd = sb("rstd", [P, TT])
        epst = sb("epst", [P, 1])
        n_it_t = sb("n_it_t", [1, 1], I32)
        acc = bias[:, 0:16, :].rearrange("q h k -> q (h k)").rearrange("q (t d) -> q t d", t=TT)
        buckets = S[0:T5_BUCKETS, 0, :, :].rearrange("q a b -> q (a b)")[:, 0:VEC]
        t5t = S[0:T5_BUCKETS, 1, 0, 0:HA]
        relt = PT[:, 0, 0, 0:3 * HB].rearrange("q (a h) -> q a h", a=3)
        flip = PT[:, 0, 1, :]
        vecA = PT[0:HA, 1, 0:3, :].rearrange("h a b -> h (a b)")
        vecB = gates[0:HB, 0, 0:2, :].rearrange("h a b -> h (a b)")[:, 0:VEC]
        pnat = S[:, 0, :, :]
        pT = PT[:, 0, :, :].rearrange("q (k t) c -> q k (t c)", k=2)
        g1 = VB[:, :, :].rearrange("q t d -> q (t d)")
        b1 = QKT[:, 16:24, :].rearrange("q a b -> q (a b)")
        g2 = QKT[:, 0:8, :].rearrange("q a b -> q (a b)")
        b2 = QKT[:, 8:16, :].rearrange("q a b -> q (a b)")
        rt = gates[:, 1, 8, :]
        sig = gates[:, 1, 9:13, :].rearrange("q a b -> q (a b)").rearrange("q (t n) -> q t n", t=TT)
        XG = gates[:, 0, 0:8, :].rearrange("q a b -> q (a b)").rearrange("q (k s) -> q k s", k=KT)
        Y = gates[:, 0, 8:16, :].rearrange("q a b -> q (a b)")
        HS = gates[:, 1, 0:4, :].rearrange("q a b -> q (a b)")
        HT = gates[:, 1, 4:8, :].rearrange("q a b -> q (a b)").rearrange("q (k s) -> q k s", k=FF // P)
        CT = gates[:, 1, 13, :]
        OH = gates[:, 1, 14, :].rearrange("q (t e s) -> q t e s", t=TT, e=2)
        OHW = gates[:, 1, 15, :].rearrange("q (t e s) -> q t e s", t=TT, e=2)
        ones = PT[:, 1, 0, :]

        r_ex, r_pr = rt[:, 0:32], rt[:, 32:64]
        r_sel, r_rank = rt[:, 64:96], rt[:, 96:128]
        r_g, r_mask = rt[:, 128:160], rt[:, 160:192]
        r_gs, r_gr = rt[:, 192:200], rt[:, 200:208]
        r_gg, r_gm = rt[:, 208:216], rt[:, 216:224]
        r_m, r_s, r_w = rt[:, 224:226], rt[:, 226:228], rt[:, 228:230]
        r_c, r_c3 = rt[:, 230:231], rt[:, 231:234]

        PS = ctx.enter_context(nc.psum_tensor("PS", [P, 8, 512], F32))
        B_LOGIT, B_PT, B_Y = 4, 6, 7
        B_H1, B_H3, B_Y4 = 0, 2, 4

        scratch = nc.dram_tensor("bias_vectors", [HA + HB, VEC], F32, kind="Internal").ap()

        weights_in = [sem(f"weights_in{s}") for s in range(RING)]
        weights_used = sem("weights_used")
        x_in = sem("x_in")
        const_in = sem("const_in")
        table_in = sem("table_in")
        small_in = sem("small_in")
        vec_ready = sem("vec_ready")
        vec_out = sem("vec_out")
        bias_in = sem("bias_in")
        bias_masked = sem("bias_masked")
        sink_ready = sem("sink_ready")
        vec_ps = sem("vec_ps")
        xt_ps = sem("xt_ps")
        xt_act, xt_dve = sem("xt_act"), sem("xt_dve")
        ev_act, ev_dve = sem("ev_act"), sem("ev_dve")
        logits_ps = sem("logits_ps")
        dve_step = sem("dve_step")
        max_ready, exp_ready, rden_ready, probs_ready = sem("max_ready"), sem("exp_ready"), sem("rden_ready"), sem("probs_ready")
        pt_ps, pt_ready, y_ps, y_ready = sem("pt_ps"), sem("pt_ready"), sem("y_ps"), sem("y_ready")
        gate_sig, merged = sem("gate_sig"), sem("merged")
        p_in, p_ps, p_ready = sem("p_in"), sem("p_ps"), sem("p_ready")
        ln_in = sem("ln_in")
        ln2_in = sem("ln2_in")
        var_ready, std_ready, norm_ready = sem("var_ready"), sem("std_ready"), sem("norm_ready")
        gain_ready = sem("gain_ready")
        x1_ready = sem("x1_ready")
        router_ps, rmax_ready, rexp_ready, mask_ready, pos_ps, routed = (
            sem("router_ps"), sem("rmax_ready"), sem("rexp_ready"), sem("mask_ready"), sem("pos_ps"), sem("routed"))
        sig_ready, acc_written = sem("sig_ready"), sem("acc_written")
        onehot_ready, gathered, xg_act, xg_dve = sem("onehot_ready"), sem("gathered"), sem("xg_act"), sem("xg_dve")
        silu_ready, h_ready, y_act, y_dve = sem("silu_ready"), sem("h_ready"), sem("y_act"), sem("y_dve")
        ht_ps, ht_act, ht_dve = sem("ht_ps"), sem("ht_act"), sem("ht_dve")
        spread_ready, ct_ps, ct_ready = sem("spread_ready"), sem("ct_ps"), sem("ct_ready")
        sum_ps = sem("sum_ps")
        out_ready, out_done = sem("out_ready"), sem("out_done")

        block = ctx.enter_context(nc.Block())

        def slot(k):
            return ring[:, k % RING, :]

        def slot_kn(k, n):
            return slot(k).rearrange("q (k n) -> q k n", n=n)

        @block.sync
        def _(sp):
            def load(k, src, width):
                if k >= RING:
                    sp.wait_ge(weights_used, k - RING + 1)
                sp.dma_start(slot_kn(k, width), src).then_inc(weights_in[k % RING], 16)

            def rows(w, k0, nk, c0, width):
                return w[k0 * P:(k0 + nk) * P, c0:c0 + width].rearrange("(k p) n -> p k n", p=P)

            for c in range(N_KVA):
                load(K_KVA + c, rows(w_in[0], 8 * c, 8, C_KA, 2 * KVA * HD), 2 * KVA * HD)
            k = K_Q
            for c0 in (C_QA, C_QA + PANEL, C_QB, C_QB + PANEL, C_KB, C_KB + PANEL, C_VB, C_VB + PANEL,
                       *(C_GA + PANEL * j for j in range(2 * NP_))):
                for q in range(4):
                    load(k, rows(w_in[0], 4 * q, 4, c0, PANEL), PANEL)
                    k += 1
            for j in range(NP_):
                for w in (w_pa, w_pb):
                    for q in range(2):
                        load(k, rows(w[0], 4 * q, 4, PANEL * j, PANEL), PANEL)
                        k += 1
            for c in range(N_PLE):
                load(k, rows(w_ple[0], 0, 2, 1024 * c, 1024), 1024)
                k += 1
            for w in (w_o, w_ple_gate):
                for j in range(NP_):
                    for q in range(4):
                        load(k, rows(w[0], 4 * q, 4, PANEL * j, PANEL), PANEL)
                        k += 1
            assert k == K_MOE

            def pair_loads(pair, it):
                for c in range(PAIR):
                    m, q, e = c // (2 * W1C), c // 2 % W1C, c % 2
                    expert = bass.ds(pair * 2 + e, 1)
                    if m < 2:
                        src = (w1, w3)[m][0][expert, 2 * P * q:2 * P * (q + 1), :].rearrange("e (k p) n -> p (e k) n", p=P)
                        dst = slot_kn(K_MOE + c, FF)
                    else:
                        src = w2[0][expert, P * q:P * (q + 1), :].rearrange("e (k p) n -> p (e k) n", p=P)
                        dst = slot_kn(K_MOE + c, D)
                    sp.wait_ge(weights_used, it * PAIR + (K_MOE + (c - RING) // 2 * 2 + 2))
                    sp.dma_start(dst, src).then_inc(weights_in[(K_MOE + c) % RING], 16)

            with sp.Fori(0, NPAIR) as pair:
                pair_loads(pair, pair)
            sp.wait_ge(routed, 1)
            n_it = sp.value_load(n_it_t[0:1, 0:1], min_val=NPAIR, max_val=NPAIR * MAXPASS)
            with sp.If(n_it > NPAIR):
                with sp.Fori(NPAIR, n_it, NPAIR) as first:
                    with sp.Fori(0, NPAIR) as pair:
                        pair_loads(pair, first + pair)

        @block.gpsimd
        def _(pool):
            for s in range(32):
                kt = s % 2 + 1
                pool.wait_ge(rden_ready, s + 1)
                for sub in range(2):
                    last = pool.tensor_scalar(S[:, s % 2, sub, 0:kt * P], S[:, s % 2, sub, 0:kt * P],
                                              rden[:, s % 2, sub:sub + 1], None, ALU.mult)
                last.then_inc(probs_ready, 1)

        @block.scalar
        def _(act):
            for t in range(TT):
                act.dma_start(X[:, t, :], x[0, t * P:(t + 1) * P, :]).then_inc(x_in, 16)
            act.dma_start(ident[:, :], square[:, 0:P]).then_inc(const_in, 16)
            act.dma_start(tri[:, :], square[:, P:2 * P]).then_inc(const_in, 16)
            act.dma_start(slots[:, :], square[:, 3 * P:]).then_inc(const_in, 16)
            act.dma_start(flip, square[:, 2 * P:3 * P]).then_inc(const_in, 16)
            act.dma_start(buckets, bucket[:, :]).then_inc(table_in, 16)
            act.dma_start(t5t, t5_table[:, :]).then_inc(table_in, 16)
            act.dma_start(relt[:, 0:2, :], relb_table[0, 0:2 * P, :].rearrange("(a p) h -> p a h", p=P)).then_inc(table_in, 16)
            act.dma_start(relt[0:REL_TABLE - 2 * P, 2, :], relb_table[0, 2 * P:REL_TABLE, :]).then_inc(table_in, 16)
            act.dma_start(sink[:, :], attn_sinks.partition_broadcast(P).rearrange("p a h -> p (a h)")).then_inc(small_in, 16)
            act.dma_start(brt[:, :], b_router.partition_broadcast(P)).then_inc(small_in, 16)
            act.dma_start(WR[:, :, :], w_router.rearrange("(k p) e -> p k e", p=P)).then_inc(small_in, 16)

            for g in range(0, 8, 2):
                act.wait_ge(xt_ps, g + 1)
                act.copy(XT[:, 2 * g:2 * g + 2, :].rearrange("q a b -> q (a b)"), PS[:, g, :]).then_inc(xt_act, 1)

            act.wait_ge(vec_ready, 2)
            act.dma_start(scratch[0:HA, :], vecA).then_inc(vec_out, 16)
            act.dma_start(scratch[HA:HA + HB, :], vecB).then_inc(vec_out, 16)
            act.wait_ge(vec_out, 32)
            for g in range(4):
                band = bass.AP(tensor=scratch.tensor, offset=8 * g * VEC, ap=[[1, P], [VEC, 8], [1, SEQ]])
                act.dma_start(bias[:, 8 * g:8 * g + 8, :], band).then_inc(bias_in, 16)

            act.wait_ge(weights_used, K_Q)
            for kv in range(KVA):
                for half in range(2):
                    last = act.copy(KA[HD * half:HD * half + HD, kv, :], PS[HD * kv:HD * kv + HD, 2 * P_KVA, 0:SEQ])
                last.then_inc(ev_act, 1)

            with act.Fori(0, N_Q // RING) as body:
                for j in range(2):
                    act.wait_ge(weights_used, body * RING + (K_Q + 4 * j + 4))
                    act.copy(QKT[:, bass.ds(body * 8 + 4 * j, 2), :].rearrange("q a b -> q (a b)"),
                             PS[:, 2 * ((P_Q + j) % 2), :]).then_inc(ev_act, 1)
            for j in range(2):
                act.wait_ge(weights_used, K_V + 4 * j + 4)
                act.copy(VB[:, 0, PANEL * j:PANEL * (j + 1)], PS[:, 2 * ((P_V + j) % 2), :]).then_inc(ev_act, 1)

            def exps(s):
                act.wait_ge(max_ready, s + 1)
                kt = s % 2 + 1
                for sub in range(2):
                    last = act.activation(S[:, s % 2, sub, 0:kt * P], S[:, s % 2, sub, 0:kt * P], ACT.Exp,
                                          bias=nmax[:, s % 2, sub:sub + 1], accum_out=esum[:, s % 2, sub:sub + 1])
                if s < 16:
                    last = act.activation(esink[:, s % 2, :], esink[:, s % 2, :], ACT.Exp)
                last.then_inc(exp_ready, 1)

            def pt_copy(s):
                act.wait_ge(pt_ps, s + 1)
                kt = s % 2 + 1
                act.copy(PT[:, s % 2, 0:2 * kt, :].rearrange("q a b -> q (a b)"),
                         PS[:, B_PT, 0:2 * kt * P]).then_inc(pt_ready, 1)

            for s in range(33):
                if s >= 1:
                    pt_copy(s - 1)
                if s < 32:
                    exps(s)
                if s % 4 == 3:
                    j = s // 4
                    act.wait_ge(weights_used, K_G + 4 * j + 4)
                    act.copy(gates[:, j // 4, 4 * (j % 4):4 * (j % 4) + 2, :].rearrange("q a b -> q (a b)"),
                             PS[:, 2 * ((P_G + j) % 2), :]).then_inc(ev_act, 1)
            act.wait_ge(y_ready, 32)
            act.dma_start(g1, ln1_g.partition_broadcast(P).rearrange("p a d -> p (a d)")).then_inc(ln_in, 16)
            act.dma_start(b1, ln1_b.partition_broadcast(P).rearrange("p a d -> p (a d)")).then_inc(ln_in, 16)
            act.dma_start(pnat, p[0, 0].rearrange("(t q) c -> q t c", q=P)).then_inc(p_in, 16)

            act.wait_ge(ev_dve, P_M)
            act.wait_ge(ev_act, P_M)
            for j in range(NP_):
                for br in range(2):
                    g = gates[:, br, 4 * j:4 * j + 4, :].rearrange("q a b -> q (a b)")
                    act.activation(g, g, ACT.Sigmoid).then_inc(gate_sig, 1)
            act.wait_ge(p_ps, 1)
            act.copy(pT.rearrange("q k t -> q (k t)"), PS[:, B_PT, :]).then_inc(p_ready, 1)
            act.wait_ge(weights_used, K_PLE)
            act.dma_start(g2, ln2_g.partition_broadcast(P).rearrange("p a d -> p (a d)")).then_inc(ln2_in, 16)
            act.dma_start(b2, ln2_b.partition_broadcast(P).rearrange("p a d -> p (a d)")).then_inc(ln2_in, 16)

            def layer_norm(r, n):
                act.wait_ge(var_ready, n)
                act.activation(rstd[:, :], mv[:, :, 1], ACT.Sqrt, bias=epst[:, 0:1]).then_inc(std_ready, 1)

            layer_norm(X, 1)

            for g in range(0, 8, 2):
                act.wait_ge(xt_ps, 8 + g + 1)
                act.copy(XT[:, 2 * g:2 * g + 2, :].rearrange("q a b -> q (a b)"), PS[:, g, :]).then_inc(xt_act, 1)

            act.wait_ge(rmax_ready, 1)
            for t in range(TT):
                last = act.activation(r_ex[:, NE * t:NE * t + NE], PS[:, B_LOGIT, NE * t:NE * t + NE], ACT.Exp,
                                      bias=r_m[:, t:t + 1], accum_out=r_s[:, t:t + 1])
            last.then_inc(rexp_ready, 1)

            for j in range(NP_):
                act.wait_ge(weights_used, K_PG + 4 * j + 4)
                if j >= 1:
                    act.wait_ge(acc_written, j)
                act.activation(sig, PS[:, 2 * ((P_PG + j) % 2):2 * ((P_PG + j) % 2) + 2, :], ACT.Sigmoid).then_inc(sig_ready, 1)

            act.wait_ge(routed, 1)
            n_it = act.value_load(n_it_t[0:1, 0:1], min_val=NPAIR, max_val=NPAIR * MAXPASS)

            def gathered_copy(it):
                act.wait_ge(gathered, it + 1)
                act.copy(XG[:, 0:8, :].rearrange("q k s -> q (k s)"),
                         PS[:, 0:2, :].rearrange("q a b -> q (a b)")).then_inc(xg_act, 1)

            def ct_copy(it):
                act.wait_ge(ct_ps, it + 1)
                act.copy(CT, PS[:, B_Y4, 0:SEQ]).then_inc(ct_ready, 1)

            gathered_copy(0)
            with act.Fori(0, n_it) as it:
                ct_copy(it)
                for f in range(2):
                    act.wait_ge(weights_used, it * PAIR + (K_MOE + 2 * W1C))
                    act.activation(HS[:, PANEL * f:PANEL * f + PANEL], PS[:, B_H1 + f, :], ACT.Silu).then_inc(silu_ready, 1)
                act.wait_ge(ht_ps, it * 2 + 1)
                act.copy(HT[:, 0:4, :].rearrange("q k s -> q (k s)"), PS[:, B_H1, :]).then_inc(ht_act, 1)
                gathered_copy(it + 1)
                act.wait_ge(weights_used, it * PAIR + (K_MOE + PAIR))
                act.copy(Y[:, 0:2 * PANEL], PS[:, B_Y4:B_Y4 + 2, :].rearrange("q a b -> q (a b)")).then_inc(y_act, 1)
            ct_copy(n_it)

            layer_norm(acc, 2)
            for t in range(TT):
                act.wait_ge(out_ready, t + 1)
                act.dma_start(out[0, t * P:(t + 1) * P, :], acc[:, t, :]).then_inc(out_done, 16)
            act.wait_ge(out_done, 16 * TT)

        @block.tensor
        def _(pe):
            def arrived(k, more=0):
                pe.wait_ge(weights_in[k % RING], more * 16 + 16 * (k // RING + 1))

            def bank_pair(n):
                return PS[:, 2 * (n % 2):2 * (n % 2) + 2, :]

            def columns(k, ps, rhs, first, last, w=PANEL):
                n = CW // w
                o = ps.rearrange("q a (b t) -> q (a b) t", t=SEQ)
                for q in range(n):
                    for m in range(4):
                        mm = pe.matmul(o[:, m, :], slot_kn(k, w)[:, q, P * m:P * m + P], rhs(q),
                                       start=(first and q == 0 and m % 2 == 0), stop=(last and q == n - 1),
                                       skip_group_check=True)
                mm.then_inc(weights_used, 1)

            def tokens(k, ps, lhs, first, last):
                for q in range(4):
                    for t in range(TT):
                        mm = pe.matmul(ps[:, t, :], lhs(q, t), slot_kn(k, PANEL)[:, q, :],
                                       start=(first and q == 0), stop=(last and q == 3), skip_group_check=True)
                mm.then_inc(weights_used, 1)

            def transpose_x(done):
                for g in range(8):
                    for b in range(4):
                        k, t = 2 * g + b // 2, b % 2
                        mm = pe.transpose(PS[:, g, P * b:P * b + P], X[:, t, P * k:P * k + P], ident[:, :])
                    mm.then_inc(xt_ps, 1)

            pe.wait_ge(x_in, 16 * TT)
            pe.wait_ge(const_in, 64)
            transpose_x(0)
            pe.wait_ge(xt_act, 4)
            pe.wait_ge(xt_dve, 4)
            pe.wait_ge(table_in, 64)
            pe.matmul(PS[0:HA, B_LOGIT, 0:VEC], t5t, buckets, start=True, stop=True)
            for a in range(3):
                n = min(P, REL_TABLE - P * a)
                mm = pe.matmul(PS[0:HB, B_LOGIT + 1, P * (3 - a) - n:P * (3 - a)], relt[0:n, a, :], flip[0:n, P - n:P],
                               start=True, stop=True)
            mm.then_inc(vec_ps, 1)

            for c in range(N_KVA):
                arrived(K_KVA + c)
                w = slot_kn(K_KVA + c, 2 * KVA * HD)
                for q in range(8):
                    k = 8 * c + q
                    pe.matmul(PS[:, 2 * P_KVA, 0:SEQ], w[:, q, 0:P], XT[:, k, :], start=(k == 0), stop=(k == KT - 1))
                    for t in range(TT):
                        mm = pe.matmul(PS[:, 2 * P_KVA + 1, P * t:P * t + P], XT[:, k, P * t:P * t + P], w[:, q, P:2 * P],
                                       start=(k == 0 and t == 0), stop=(k == KT - 1), skip_group_check=True)
                mm.then_inc(weights_used, 1)

            with pe.Fori(0, N_Q // RING) as body:
                for j in range(2):
                    pe.wait_ge(ev_act, body * 2 + (P_Q + j - 1))
                    pe.wait_ge(ev_dve, body * 2 + (P_Q + j - 1))
                    for c in range(4):
                        k = K_Q + 4 * j + c
                        arrived(k, body)
                        columns(k, bank_pair(P_Q + j), lambda q, c=c: XT[:, 4 * c + q, :], c == 0, c == 3)
            for j in range(2):
                pe.wait_ge(ev_act, P_V + j - 1)
                pe.wait_ge(ev_dve, P_V + j - 1)
                for c in range(4):
                    k = K_V + 4 * j + c
                    arrived(k)
                    tokens(k, bank_pair(P_V + j), lambda q, t, c=c: XT[:, 4 * c + q, P * t:P * t + P], c == 0, c == 3)

            def logits(s):
                br, i, t = s // 16, s % 16 // 2, s % 2
                keys = P * (t + 1)
                pe.wait_ge(max_ready, s)
                for sub in range(2):
                    h = slice(HD * sub, HD * sub + HD)
                    rhs = KA[h, i // 4, 0:keys] if br == 0 else QKT[h, 16 + i, 0:keys]
                    mm = pe.matmul(PS[:, B_LOGIT + sub, 0:keys], QKT[h, 8 * br + i, P * t:P * t + P],
                                   rhs, start=True, stop=True)
                mm.then_inc(logits_ps, 1)

            def transposes(s):
                t = s % 2
                pe.wait_ge(probs_ready, s + 1)
                pe.wait_ge(pt_ready, s)
                for sub in range(2):
                    for k in range(t + 1):
                        n = sub * (t + 1) + k
                        mm = pe.transpose(PS[:, B_PT, P * n:P * n + P], S[:, s % 2, sub, P * k:P * k + P], ident[:, :])
                mm.then_inc(pt_ps, 1)

            def values(s):
                br, i, t = s // 16, s % 16 // 2, s % 2
                pe.wait_ge(pt_ready, s + 1)
                pe.wait_ge(y_ready, s)
                for sub in range(2):
                    for k in range(t + 1):
                        v = VA[:, k, HD * (i // 4):HD * (i // 4) + HD] if br == 0 else VB[:, k, HD * (2 * i + sub):HD * (2 * i + sub + 1)]
                        mm = pe.matmul(PS[0:HD, B_Y, P * sub:P * sub + P], v, PT[:, s % 2, sub * (t + 1) + k, :],
                                       start=(k == 0), stop=(k == t))
                mm.then_inc(y_ps, 1)

            pe.wait_ge(bias_masked, 1)
            pe.wait_ge(ev_act, P_G - 1)
            pe.wait_ge(ev_dve, P_G - 1)
            for s in range(34):
                if s == 1:
                    pe.wait_ge(ev_act, P_G)
                    pe.wait_ge(ev_dve, P_G)
                if s < 32:
                    logits(s)
                if 1 <= s <= 32:
                    transposes(s - 1)
                if 2 <= s:
                    values(s - 2)
                if s < 32:
                    j, c = s // 4, s % 4
                    if c == 0:
                        pe.wait_ge(ev_act, P_G + j - 1)
                        pe.wait_ge(ev_dve, P_G + j - 1)
                    arrived(K_G + s)
                    columns(K_G + s, bank_pair(P_G + j), lambda q, c=c: XT[:, 4 * c + q, :], c == 0, c == 3)

            pe.wait_ge(y_ready, 32)
            pe.wait_ge(ev_act, P_M)
            with pe.Fori(0, N_M // RING) as body:
                for n in range(4):
                    pe.wait_ge(ev_dve, body * 4 + (P_M + n - 1))
                    for c in range(2):
                        k = K_M + 2 * n + c
                        arrived(k, body)
                        columns(k, bank_pair(P_M + n), lambda q, c=c, n=n: QKT[:, 8 * (n % 2) + 4 * c + q, :], c == 0, c == 1)

            pe.wait_ge(p_in, 16)
            for k in range(2):
                for t in range(TT):
                    mm = pe.transpose(PS[:, B_PT, P * (2 * k + t):P * (2 * k + t) + P], pnat[:, t, P * k:P * k + P], ident[:, :])
            mm.then_inc(p_ps, 1)
            pe.wait_ge(p_ready, 1)
            for c in range(N_PLE):
                k = K_PLE + c
                arrived(k)
                for j in range(2):
                    n = P_PLE + 2 * c + j
                    pe.wait_ge(ev_dve, n - 1)
                    for q in range(2):
                        for t in range(TT):
                            mm = pe.matmul(bank_pair(n)[:, t, :], pT[:, q, P * t:P * t + P],
                                           slot_kn(k, 1024)[:, q, PANEL * j:PANEL * j + PANEL], start=(q == 0), stop=(q == 1))
                mm.then_inc(weights_used, 1)

            pe.wait_ge(merged, NP_)
            with pe.Fori(0, N_O // RING) as body:
                for j in range(2):
                    pe.wait_ge(ev_dve, body * 2 + (P_O + j - 1))
                    for c in range(4):
                        k = K_O + 4 * j + c
                        arrived(k, body)
                        tokens(k, bank_pair(P_O + j), lambda q, t, c=c: gates[:, 0, 4 * c + q, P * t:P * t + P], c == 0, c == 3)

            pe.wait_ge(x1_ready, 1)
            transpose_x(1)
            pe.wait_ge(xt_act, 8)
            pe.wait_ge(xt_dve, 8)
            pe.wait_ge(small_in, 48)
            for t in range(TT):
                for k in range(KT):
                    mm = pe.matmul(PS[:, B_LOGIT, NE * t:NE * t + NE], XT[:, k, P * t:P * t + P], WR[:, k, :],
                                   start=(k == 0), stop=(k == KT - 1))
            mm.then_inc(router_ps, 1)

            def positions():
                pe.wait_ge(mask_ready, 1)
                m = r_mask.rearrange("q (t e) -> q t e", t=TT)
                o = PS[:, B_LOGIT + 1, 0:3 * NE].rearrange("q (t e) -> q t e", e=NE)
                pe.matmul(o[:, 0, :], tri[:, :], m[:, 0, :], start=True, stop=True)
                pe.matmul(o[:, 1, :], ones, m[:, 0, :], start=True, stop=False)
                pe.matmul(o[:, 1, :], tri[:, :], m[:, 1, :], start=False, stop=True)
                pe.matmul(o[:, 2, :], ones, m[:, 0, :], start=True, stop=False)
                pe.matmul(o[:, 2, :], ones, m[:, 1, :], start=False, stop=True).then_inc(pos_ps, 1)

            for j in range(NP_):
                if j == 1:
                    positions()
                if j >= 2:
                    pe.wait_ge(sig_ready, j - 1)
                for c in range(4):
                    k = K_PG + 4 * j + c
                    arrived(k)
                    tokens(k, bank_pair(P_PG + j), lambda q, t, c=c: XT[:, 4 * c + q, P * t:P * t + P], c == 0, c == 3)

            pe.wait_ge(routed, 1)
            n_it = pe.value_load(n_it_t[0:1, 0:1], min_val=NPAIR, max_val=NPAIR * MAXPASS)
            pe.wait_ge(sig_ready, NP_)

            def gather(it):
                pe.wait_ge(onehot_ready, it + 1)
                o = PS[:, 0:4, :].rearrange("q a (k s) -> q (a k) s", s=2 * SLOTS)
                for k in range(KT):
                    for t in range(TT):
                        mm = pe.matmul(o[:, k, :], X[:, t, P * k:P * k + P], OH[:, t, :, :].rearrange("q e s -> q (e s)"),
                                       start=(k % 4 == 0 and t == 0), stop=(t == TT - 1), skip_group_check=True)
                mm.then_inc(gathered, 1)

            def up(it, m, c):
                for e in range(2):
                    arrived(K_MOE + 2 * (W1C * m + c) + e, it * (PAIR // RING))
                for q in range(2):
                    for f in range(2):
                        for e in range(2):
                            k = K_MOE + 2 * (W1C * m + c) + e
                            mm = pe.matmul(PS[SLOTS * e:SLOTS * e + SLOTS, (B_H1, B_H3)[m] + f, :],
                                           XG[:, 2 * c + q, SLOTS * e:SLOTS * e + SLOTS],
                                           slot_kn(k, FF)[:, q, PANEL * f:PANEL * f + PANEL],
                                           start=(c == 0 and q == 0), stop=(c == W1C - 1 and q == 1), skip_group_check=True)
                mm.then_inc(weights_used, 2)

            def down(it, c):
                for e in range(2):
                    arrived(K_MOE + 4 * W1C + 2 * c + e, it * (PAIR // RING))
                for j in range(NP_):
                    for e in range(2):
                        k = K_MOE + 4 * W1C + 2 * c + e
                        mm = pe.matmul(PS[SLOTS * e:SLOTS * e + SLOTS, B_Y4 + j, :], HT[:, c, SLOTS * e:SLOTS * e + SLOTS],
                                       slot(k)[:, PANEL * j:PANEL * j + PANEL],
                                       start=(c == 0), stop=(c == W1C - 1), skip_group_check=True)
                mm.then_inc(weights_used, 2)

            def turn_hidden(it):
                for f in range(2):
                    pe.wait_ge(h_ready, it * 2 + (f + 1))
                    for b in range(4):
                        mm = pe.transpose(PS[:, B_H1 + f, P * b:P * b + P], HS[:, PANEL * f + P * b:PANEL * f + P * b + P], ident[:, :])
                    mm.then_inc(ht_ps, 1)

            def spread_matrix(it):
                pe.wait_ge(spread_ready, it + 1)
                pe.wait_ge(y_act, it + 1)
                pe.wait_ge(y_dve, it + 1)
                for t in range(TT):
                    mm = pe.transpose(PS[:, B_Y4, P * t:P * t + P], OHW[:, t, :, :].rearrange("q e s -> q (e s)"), ident[:, :])
                mm.then_inc(ct_ps, 1)

            def spread(it, n):
                if n == 0:
                    pe.wait_ge(ct_ready, it + 1)
                pe.wait_ge(acc_written, it * 8 + (NP_ + max(n - 3, 0)))
                pe.matmul(PS[:, B_Y4 + n % 4, :], CT[:, P * (n // 4):P * (n // 4) + P], Y[:, PANEL * (n % 4):PANEL * (n % 4) + PANEL],
                          start=True, stop=True).then_inc(sum_ps, 1)

            gather(0)
            with pe.Fori(0, n_it) as it:
                spread_matrix(it)
                pe.wait_ge(xg_act, it + 1)
                pe.wait_ge(xg_dve, it + 1)
                for m in range(2):
                    for c in range(W1C):
                        up(it, m, c)
                        if c < 4:
                            spread(it, 4 * m + c)
                turn_hidden(it)
                pe.wait_ge(ht_act, it + 1)
                pe.wait_ge(ht_dve, it + 1)
                pe.wait_ge(acc_written, it * 8 + (NP_ + 8))
                for c in range(W1C):
                    down(it, c)
                    if c == 0:
                        gather(it + 1)
            spread_matrix(n_it)
            for n in range(8):
                spread(n_it, n)

        @block.vector
        def _(dve):
            steps = [0]

            def link(ins, base=0):
                steps[0] += 1
                ins.then_inc(dve_step, 1)
                dve.wait_ge(dve_step, base + steps[0])

            def bank2(n, b):
                return PS[:, 2 * (n % 2) + b, :]

            dve.memset(epst[:, :], LN_EPS)
            dve.memset(vecB[:, 0:VEC - REL_TABLE], 0.0)
            for g in range(1, 8, 2):
                dve.wait_ge(xt_ps, g + 1)
                dve.tensor_copy(XT[:, 2 * g:2 * g + 2, :].rearrange("q a b -> q (a b)"), PS[:, g, :]).then_inc(xt_dve, 1)
            dve.wait_ge(vec_ps, 1)
            dve.tensor_copy(vecA, PS[0:HA, B_LOGIT, 0:VEC]).then_inc(vec_ready, 1)
            dve.tensor_copy(vecB[:, VEC - REL_TABLE:VEC], PS[0:HB, B_LOGIT + 1, VEC - REL_TABLE:VEC]).then_inc(vec_ready, 1)
            dve.wait_ge(small_in, 48)
            dve.tensor_scalar(nsink[:, :], sink[:, :], -1.0, None, ALU.mult).then_inc(sink_ready, 1)

            dve.wait_ge(weights_used, K_Q)
            for t in range(TT):
                dve.tensor_copy(VA[:, t, :], PS[:, 2 * P_KVA + 1, P * t:P * t + P]).then_inc(ev_dve, 1)
            with dve.Fori(0, N_Q // RING) as body:
                for j in range(2):
                    dve.wait_ge(weights_used, body * RING + (K_Q + 4 * j + 4))
                    dve.tensor_copy(QKT[:, bass.ds(body * 8 + 4 * j + 2, 2), :].rearrange("q a b -> q (a b)"),
                                    bank2(P_Q + j, 1)).then_inc(ev_dve, 1)
            dve.wait_ge(bias_in, 64)
            dve.memset(bias[0:CHUNK, 0:HA, 3 * CHUNK:SEQ], NEG)
            dve.memset(bias[CHUNK:P, 0:HA, P:SEQ], NEG)
            dve.memset(bias[0:CHUNK, :, 0:CHUNK], NEG).then_inc(bias_masked, 1)
            for j in range(2):
                dve.wait_ge(weights_used, K_V + 4 * j + 4)
                dve.tensor_copy(VB[:, 1, PANEL * j:PANEL * (j + 1)], bank2(P_V + j, 1)).then_inc(ev_dve, 1)

            dve.wait_ge(bias_masked, 1)
            dve.wait_ge(sink_ready, 1)

            def biased(s):
                br, i, t = s // 16, s % 16 // 2, s % 2
                keys, b = P * (t + 1), s % 2
                dve.wait_ge(logits_ps, s + 1)
                if s >= 2:
                    dve.wait_ge(pt_ps, s - 1)
                ps = PS[:, B_LOGIT:B_LOGIT + 2, 0:keys]
                h0 = HA * br + 2 * i
                link(dve.scalar_tensor_tensor(out=S[:, b, :, 0:keys], in0=ps, scalar=SCALE,
                                              in1=bias[:, h0:h0 + 2, 0:keys][:, :, ::-1], op0=ALU.mult, op1=ALU.add))
                if br == 1:
                    dve.tensor_reduce(nmax[:, b, :], S[:, b, :, 0:keys], AX.X, ALU.max, negate=True).then_inc(max_ready, 1)
                else:
                    link(dve.tensor_reduce(nmax[:, b, :], S[:, b, :, 0:keys], AX.X, ALU.max, negate=True))
                    link(dve.tensor_tensor(nmax[:, b, :], nmax[:, b, :], nsink[:, 2 * i:2 * i + 2], ALU.min))
                    dve.tensor_tensor(esink[:, b, :], sink[:, 2 * i:2 * i + 2], nmax[:, b, :], ALU.add).then_inc(max_ready, 1)

            def denominators(s):
                b = s % 2
                dve.wait_ge(exp_ready, s + 1)
                if s < 16:
                    link(dve.tensor_tensor(esum[:, b, :], esum[:, b, :], esink[:, b, :], ALU.add))
                dve.reciprocal(rden[:, b, :], esum[:, b, :]).then_inc(rden_ready, 1)

            def outputs(s):
                br, i, t = s // 16, s % 16 // 2, s % 2
                dve.wait_ge(y_ps, s + 1)
                for sub in range(2):
                    last = dve.tensor_copy(QKT[HD * sub:HD * sub + HD, 8 * br + i, P * t:P * t + P],
                                           PS[0:HD, B_Y, P * sub:P * sub + P])
                last.then_inc(y_ready, 1)

            for s in range(34):
                if s < 32:
                    biased(s)
                    denominators(s)
                if s >= 2:
                    outputs(s - 2)
                if s < 32 and s % 4 == 3:
                    j = s // 4
                    dve.wait_ge(weights_used, K_G + 4 * j + 4)
                    dve.tensor_copy(gates[:, j // 4, 4 * (j % 4) + 2:4 * (j % 4) + 4, :].rearrange("q a b -> q (a b)"),
                                    bank2(P_G + j, 1)).then_inc(ev_dve, 1)

            for j in range(NP_):
                for br in range(2):
                    n = 2 * j + br
                    g = gates[:, br, 4 * j:4 * j + 4, :].rearrange("q a b -> q (a b)")
                    dve.wait_ge(gate_sig, n + 1)
                    dve.wait_ge(weights_used, K_M + 2 * n + 2)
                    ins = dve.tensor_tensor(g, PS[:, 2 * ((P_M + n) % 2):2 * ((P_M + n) % 2) + 2, :].rearrange("q a b -> q (a b)"), g, ALU.mult)
                    ins.then_inc(ev_dve, 1)
                dve.wait_ge(ev_dve, P_M + 2 * j + 2)
                ga = gates[:, 0, 4 * j:4 * j + 4, :].rearrange("q a b -> q (a b)")
                dve.tensor_tensor(ga, ga, g, ALU.add).then_inc(merged, 1)
            for n in range(NP_):
                dve.wait_ge(weights_used, K_PLE + n // 2 + 1)
                dve.tensor_copy(acc[:, :, PANEL * n:PANEL * n + PANEL],
                                PS[:, 2 * ((P_PLE + n) % 2):2 * ((P_PLE + n) % 2) + 2, :]).then_inc(ev_dve, 1)
            for j in range(NP_):
                dve.wait_ge(weights_used, K_O + 4 * j + 4)
                xs = X[:, :, PANEL * j:PANEL * j + PANEL]
                dve.scalar_tensor_tensor(out=xs, in0=xs, scalar=ALPHA,
                                         in1=PS[:, 2 * ((P_O + j) % 2):2 * ((P_O + j) % 2) + 2, :],
                                         op0=ALU.mult, op1=ALU.add).then_inc(ev_dve, 1)
                dve.wait_ge(ev_dve, P_O + j + 1)
                for t in range(TT):
                    last = dve.bn_stats(stats[:, t, j, :], X[:, t, PANEL * j:PANEL * j + PANEL])
            link(last)

            def normalise(r, n, g, b, done, vectors):
                for t in range(TT):
                    last = dve.bn_aggr(mv[:, t, :], stats[:, t, :, :].rearrange("q a b -> q (a b)"))
                last.then_inc(var_ready, 1)
                dve.wait_ge(std_ready, n)
                link(dve.reciprocal(rstd[:, :], rstd[:, :]))
                dve.wait_ge(vectors, 32)
                for t in range(TT):
                    link(dve.tensor_scalar(r[:, t, :], r[:, t, :], mv[:, t, 0:1], rstd[:, t:t + 1], ALU.subtract, ALU.mult))
                    link(dve.tensor_tensor(r[:, t, :], r[:, t, :], g, ALU.mult))
                    last = dve.tensor_tensor(r[:, t, :], r[:, t, :], b, ALU.add)
                    if done is out_ready:
                        last.then_inc(done, 1)
                if done is not out_ready:
                    last.then_inc(done, 1)

            normalise(X, 1, g1, b1, x1_ready, ln_in)

            dve.memset(ones, 1.0)
            dve.memset(OHW, 0.0).then_inc(spread_ready, 1)
            dve.memset(Y[:, 0:2 * PANEL], 0.0).then_inc(y_act, 1)
            dve.memset(Y[:, 2 * PANEL:], 0.0).then_inc(y_dve, 1)
            for g in range(1, 8, 2):
                dve.wait_ge(xt_ps, 8 + g + 1)
                dve.tensor_copy(XT[:, 2 * g:2 * g + 2, :].rearrange("q a b -> q (a b)"), PS[:, g, :]).then_inc(xt_dve, 1)

            def te(a):
                return a.rearrange("q (t e) -> q t e", t=TT)

            def tge(a):
                return a.rearrange("q (t e) -> q t e", e=EPG)

            def rank(val, r, g, n):
                for i in range(n):
                    last = dve.memset(r[:, :, i], float(n - 1 - i))
                link(last)
                for s in range(1, n):
                    link(dve.tensor_tensor(g[:, :, 0:n - s], val[:, :, 0:n - s], val[:, :, s:n], ALU.is_ge))
                    link(dve.tensor_tensor(r[:, :, s:n], r[:, :, s:n], g[:, :, 0:n - s], ALU.add))
                    link(dve.tensor_tensor(r[:, :, 0:n - s], r[:, :, 0:n - s], g[:, :, 0:n - s], ALU.subtract))

            def route():
                lg = te(PS[:, B_LOGIT, 0:2 * NE])
                dve.wait_ge(router_ps, 1)
                dve.tensor_reduce(r_m, lg, AX.X, ALU.max, negate=True).then_inc(rmax_ready, 1)
                dve.wait_ge(rexp_ready, 1)
                link(dve.reciprocal(r_s, r_s))
                link(dve.tensor_tensor(te(r_pr), te(r_ex), r_s.unsqueeze(2).broadcast_to([P, TT, NE]), ALU.mult))
                link(dve.tensor_tensor(te(r_sel), te(r_pr), brt[:, :].unsqueeze(1).broadcast_to([P, TT, NE]), ALU.add))
                rank(tge(r_sel), tge(r_rank), tge(r_g), EPG)
                link(dve.tensor_scalar(r_rank, r_rank, 2.0, None, ALU.is_lt))
                link(dve.tensor_tensor(r_g, r_sel, r_rank, ALU.mult))
                link(dve.tensor_reduce(r_gs, tge(r_g), AX.X, ALU.add))
                rank(tge(r_gs), tge(r_gr), tge(r_gg), NG)
                link(dve.tensor_scalar(r_gm, r_gr, 1.0, None, ALU.is_lt))
                link(dve.tensor_tensor(tge(r_mask), tge(r_rank), r_gm.unsqueeze(2).broadcast_to([P, TT * NG, EPG]), ALU.mult))
                link(dve.tensor_tensor(r_g, r_pr, r_mask, ALU.mult))
                steps[0] += 1
                last = dve.tensor_reduce(r_w, te(r_g), AX.X, ALU.add)
                last.then_inc(dve_step, 1)
                dve.wait_ge(dve_step, steps[0])
                link(dve.reciprocal(r_w, r_w))
                dve.tensor_tensor(te(r_g), te(r_g), r_w.unsqueeze(2).broadcast_to([P, TT, NE]), ALU.mult).then_inc(mask_ready, 1)
                dve.wait_ge(mask_ready, 1)
                dve.memset(wsel[:, :, MAXPASS * NE:], 0.0)
                dve.memset(posm[:, :, MAXPASS * NE:], -1.0)
                for r in range(MAXPASS):
                    dve.tensor_copy(wsel[:, :, NE * r:NE * r + NE], te(r_g))
                dve.wait_ge(pos_ps, 1)
                pos = PS[:, B_LOGIT + 1, 0:3 * NE]
                link(dve.scalar_tensor_tensor(out=r_sel, in0=pos[:, 0:2 * NE], scalar=1.0, in1=r_mask, op0=ALU.add, op1=ALU.mult))
                for r in range(MAXPASS):
                    dve.tensor_scalar(posm[:, :, NE * r:NE * r + NE], te(r_sel), -1.0 - SLOTS * r, None, ALU.add)
                link(dve.tensor_reduce(r_c, pos[:, 2 * NE:3 * NE], AX.X, ALU.max))
                for r in range(1, MAXPASS):
                    link(dve.tensor_scalar(r_c3[:, r - 1:r], r_c, float(SLOTS * r), float(NPAIR), ALU.is_gt, ALU.mult))
                link(dve.tensor_reduce(r_c, r_c3, AX.X, ALU.add))
                dve.tensor_scalar(n_it_t[0:1, 0:1], r_c[0:1, :], float(NPAIR), None, ALU.add).then_inc(routed, 1)

            route()

            for j in range(NP_):
                dve.wait_ge(sig_ready, j + 1)
                a = acc[:, :, PANEL * j:PANEL * j + PANEL]
                link(dve.tensor_tensor(a, a, sig, ALU.mult))
                dve.scalar_tensor_tensor(out=a, in0=X[:, :, PANEL * j:PANEL * j + PANEL], scalar=ALPHA, in1=a,
                                         op0=ALU.mult, op1=ALU.add).then_inc(acc_written, 1)

            dve.wait_ge(routed, 1)
            n_it = dve.value_load(n_it_t[0:1, 0:1], min_val=NPAIR, max_val=NPAIR * MAXPASS)

            def onehots(it2):
                for e in range(2):
                    for t in range(TT):
                        last = dve.tensor_scalar(OH[:, t, e, :], slots[:, :], posm[:, t, bass.ds(it2 + e, 1)], None, ALU.is_equal)
                last.then_inc(onehot_ready, 1)

            def spread_weights(it2):
                for e in range(2):
                    for t in range(TT):
                        last = dve.tensor_scalar(OHW[:, t, e, :], slots[:, :], posm[:, t, bass.ds(it2 + e, 1)],
                                                 wsel[:, t, bass.ds(it2 + e, 1)], ALU.is_equal, ALU.mult)
                last.then_inc(spread_ready, 1)

            def gathered_copy(it):
                dve.wait_ge(gathered, it + 1)
                dve.tensor_copy(XG[:, 8:16, :].rearrange("q k s -> q (k s)"),
                                PS[:, 2:4, :].rearrange("q a b -> q (a b)")).then_inc(xg_dve, 1)

            def add_sum(it, n):
                t, j = n // 4, n % 4
                a = acc[:, t, PANEL * j:PANEL * j + PANEL]
                dve.wait_ge(sum_ps, it * 8 + (n + 1))
                dve.tensor_tensor(a, PS[:, B_Y4 + j, :], a, ALU.add).then_inc(acc_written, 1)

            dve.wait_ge(acc_written, NP_)
            onehots(0)
            gathered_copy(0)
            with dve.Fori(0, n_it) as it:
                for n in range(8):
                    add_sum(it, n)
                for f in range(2):
                    h = HS[:, PANEL * f:PANEL * f + PANEL]
                    dve.wait_ge(weights_used, it * PAIR + (K_MOE + 4 * W1C))
                    dve.wait_ge(silu_ready, it * 2 + (f + 1))
                    dve.tensor_tensor(h, PS[:, B_H3 + f, :], h, ALU.mult).then_inc(h_ready, 1)
                onehots(it * 2 + 2)
                spread_weights(it * 2)
                dve.wait_ge(ht_ps, it * 2 + 2)
                dve.tensor_copy(HT[:, 4:8, :].rearrange("q k s -> q (k s)"), PS[:, B_H1 + 1, :]).then_inc(ht_dve, 1)
                gathered_copy(it + 1)
                dve.wait_ge(weights_used, it * PAIR + (K_MOE + PAIR))
                dve.tensor_copy(Y[:, 2 * PANEL:], PS[:, B_Y4 + 2:B_Y4 + 4, :].rearrange("q a b -> q (a b)")).then_inc(y_dve, 1)
            for n in range(8):
                add_sum(n_it, n)

            dve.wait_ge(acc_written, n_it * 8 + (NP_ + 8))
            for t in range(TT):
                for j in range(NP_):
                    last = dve.bn_stats(stats[:, t, j, :], acc[:, t, PANEL * j:PANEL * j + PANEL])
            link(last)
            normalise(acc, 2, g2, b2, out_ready, ln2_in)


_INS = ["x", "p", "w_in", "w_pa", "w_pb", "w_o", "attn_sinks", "relb_table", "ln1_g", "ln1_b", "w_router", "b_router",
        "w1", "w3", "w2", "w_ple", "w_ple_gate", "ln2_g", "ln2_b", "t5_table"]


def kernel(**inputs):
    import concourse.bacc as bacc
    from concourse.bass_utils import run_bass_kernel_spmd

    nc = bacc.Bacc("TRN2", target_bir_lowering=False, num_devices=1)
    arrays, args = {}, []
    square, bucket = shape_constants()
    for name, a in [(n, inputs[n]) for n in _INS] + [("square", square), ("bucket", bucket)]:
        a = np.ascontiguousarray(a)
        arrays[f"in_{name}"] = a
        args.append(nc.dram_tensor(f"in_{name}", a.shape, mybir.dt.from_np(a.dtype), kind="ExternalInput").ap())
    out = nc.dram_tensor("out", (1, SEQ, D), F32, kind="ExternalOutput").ap()
    build(nc, *args, out)
    r = run_bass_kernel_spmd(nc, [arrays], core_ids=[0])
    return r.results[0]["out"]
```

```python
from contextlib import ExitStack

import concourse.bass as bass
from concourse import mybir
import numpy as np

F32 = mybir.dt.float32
F32R = mybir.dt.float32r
I32 = mybir.dt.int32
ALU = mybir.AluOpType
ACT = mybir.ActivationFunctionType
AX = mybir.AxisListType

P = 128
SEQ, D, FF, PLE = 256, 2048, 1024, 256
CHUNK, HD, HA, KVA, HB = 64, 64, 16, 2, 16
REL_CLIP, REL_TABLE = 256, 320
T5_BUCKETS, T5_MAX_DISTANCE = 32, 64
NE, NG, EPG = 16, 4, 4
ALPHA = 2.0 ** 0.25
LN_EPS = 1e-5
NEG = -1e30
SCALE = float(HD) ** -0.5

TT = SEQ // P
KT = D // P
PANEL = 512
NP_ = D // PANEL
VEC = 384

C_QA, C_KA, C_VA = 0, HA * HD, HA * HD + KVA * HD
C_QB = C_VA + KVA * HD
C_KB, C_VB = C_QB + HB * HD, C_QB + 2 * HB * HD
C_GA = C_QB + 3 * HB * HD
C_GB = C_GA + D

RING = 6
CW = 2048
N_KVA, N_Q, N_V, N_G, N_M, N_PLE, N_O = 2, 24, 8, 32, 16, 2, 16
N_PG = 4 * NP_
K_KVA = 0
K_Q = K_KVA + N_KVA
K_V = K_Q + N_Q
K_G = K_V + N_V
K_M = K_G + N_G
K_O = K_M + N_M
K_PLE = K_O + N_O
K_PG = K_PLE + N_PLE
PG_AHEAD = 1
K_MOE = K_PG + PG_AHEAD
W1C = 8
PAIR = 2 * 3 * W1C
UPS = 2 * W1C
K_LOOP = K_PG + PAIR + N_PG
LOOP_PANELS = 3
assert N_Q % (4 * LOOP_PANELS) == 0 and 4 * LOOP_PANELS % RING == PAIR % RING == 0

UNIT = CW // 4
UBUF = 4


def first_at(u):
    return 2 * u + max(0, u - PG_AHEAD)


SLOTS = 64
NPAIR = NE // 2
MAXPASS = SEQ // SLOTS
ECOLS = MAXPASS * NE + 2

P_KVA, P_Q, P_V, P_G, P_M, P_O, P_PLE = 1, 2, 8, 10, 18, 26, 30


def t5_bucket(rel):
    nb = T5_BUCKETS // 2
    ret = (rel > 0).astype(np.int32) * nb
    n = np.abs(rel)
    max_exact = nb // 2
    large = max_exact + (np.log(np.maximum(n, 1).astype(np.float32) / max_exact)
                         / np.log(T5_MAX_DISTANCE / max_exact) * (nb - max_exact)).astype(np.int32)
    return ret + np.where(n < max_exact, n, np.minimum(large, nb - 1))


def shape_constants():
    k = np.arange(P)
    square = np.zeros((P, 3 * P + SLOTS), np.float32)
    square[:, 0:P] = np.eye(P)
    square[:, P:2 * P] = k[:, None] < k[None, :]
    square[:, 2 * P:3 * P] = np.eye(P)[:, ::-1]
    square[:, 3 * P:] = np.arange(SLOTS)[None, :]
    bucket = (np.arange(T5_BUCKETS)[:, None] == t5_bucket(np.arange(VEC)[::-1] - REL_CLIP)[None, :]).astype(np.float32)
    return square, bucket


def build(nc, x, p, w_in, w_pa, w_pb, w_o, attn_sinks, relb_table, ln1_g, ln1_b, w_router, b_router,
          w1, w3, w2, w_ple, w_ple_gate, ln2_g, ln2_b, t5_table, square, bucket, out):
    with ExitStack() as ctx:
        def sb(name, shape, dt=F32):
            return ctx.enter_context(nc.sbuf_tensor(name, shape, dt))

        def sem(name):
            return ctx.enter_context(nc.semaphore(name))

        ring = sb("ring", [P, RING, CW])
        X = sb("X", [P, TT, D])
        XH = sb("XH", [P, KT, SEQ], F32R)
        XL = sb("XL", [P, KT, SEQ], F32R)
        WH = sb("WH", [P, UBUF, UNIT], F32R)
        WL = sb("WL", [P, UBUF, UNIT], F32R)
        biasB = sb("biasB", [P, HB, SEQ])
        QKT = sb("QKT", [P, 24, SEQ])
        KA = sb("KA", [P, KVA, SEQ])
        VA = sb("VA", [P, TT, KVA * HD])
        VB = sb("VB", [P, TT, HB * HD])
        gates = sb("gates", [P, 2, KT, SEQ])
        S = sb("S", [P, 2, 2, SEQ])
        PT = sb("PT", [P, 2, 4, P])
        ident = sb("ident", [P, P])
        tri = sb("tri", [P, P])
        WR2 = sb("WR2", [P, KT, 2, NE], F32R)
        nsink = sb("nsink", [P, HA])
        sink = sb("sink", [P, HA])
        brt = sb("brt", [P, NE])
        posm = sb("posm", [P, TT, ECOLS])
        wsel = sb("wsel", [P, TT, ECOLS])
        nmax = sb("nmax", [P, 2, 2])
        esum = sb("esum", [P, 2, 2])
        esink = sb("esink", [P, 2, 2])
        rden = sb("rden", [P, 2, 2])
        stats = sb("stats", [P, TT, NP_, 6])
        mv = sb("mv", [P, TT, 2])
        rstd = sb("rstd", [P, TT])
        shift = sb("shift", [P, TT])
        epst = sb("epst", [P, 1])
        n_more_t = sb("n_more_t", [1, 1], I32)
        biasA = X[:, :, :].rearrange("q t d -> q (t d)").rearrange("q (h k) -> q h k", h=HA)
        acc = biasB[:, :, :].rearrange("q h k -> q (h k)").rearrange("q (t d) -> q t d", t=TT)
        ple = QKT[:, 0:16, :].rearrange("q a b -> q (a b)").rearrange("q (t d) -> q t d", t=TT)
        WR = S[:, 1, 0, :].rearrange("q (k e) -> q k e", e=NE)
        buckets = S[0:T5_BUCKETS, 0, :, :].rearrange("q a b -> q (a b)")[:, 0:VEC]
        t5t = S[0:T5_BUCKETS, 1, 0, 0:HA]
        VAT = S[:, 1, 1, :]
        relt = PT[:, 0, 0, 0:3 * HB].rearrange("q (a h) -> q a h", a=3)
        flip = PT[:, 0, 1, :]
        vecA = PT[0:HA, 1, 0:3, :].rearrange("h a b -> h (a b)")
        vecB = gates[0:HB, 0, 0:2, :].rearrange("h a b -> h (a b)")[:, 0:VEC]
        slots = VA[:, 0, 0:SLOTS]
        pnat = S[:, 0, :, :]
        g1 = VB[:, :, :].rearrange("q t d -> q (t d)")
        b1 = QKT[:, 16:24, :].rearrange("q a b -> q (a b)")
        g2, b2 = g1, b1
        rt = gates[:, 1, 8, :]
        sig = gates[:, 1, 9:13, :].rearrange("q a b -> q (a b)").rearrange("q (t n) -> q t n", t=TT)
        XG = gates[:, 0, 0:8, :].rearrange("q a b -> q (a b)").rearrange("q (k s) -> q k s", k=KT)
        Y = gates[:, 0, 8:16, :].rearrange("q a b -> q (a b)")
        HS = gates[:, 1, 0:4, :].rearrange("q a b -> q (a b)")
        HT = gates[:, 1, 4:8, :].rearrange("q a b -> q (a b)").rearrange("q (k s) -> q k s", k=FF // P)
        CT = gates[:, 1, 13, :]
        OH = gates[:, 1, 14, :].rearrange("q (t e s) -> q t e s", t=TT, e=2)
        OHW = gates[:, 1, 15, :].rearrange("q (t e s) -> q t e s", t=TT, e=2)
        ones = PT[:, 1, 0, :]
        RL = gates[0:2 * NE, 1, 9, :]

        r_ex, r_pr = rt[:, 0:32], rt[:, 32:64]
        r_sel, r_rank = rt[:, 64:96], rt[:, 96:128]
        r_g, r_mask = rt[:, 128:160], rt[:, 160:192]
        r_gs, r_gr = rt[:, 192:200], rt[:, 200:208]
        r_gg, r_gm = rt[:, 208:216], rt[:, 216:224]
        r_m, r_s, r_w = rt[:, 224:226], rt[:, 226:228], rt[:, 228:230]
        r_c, r_c3 = rt[:, 230:231], rt[:, 231:234]

        PS = ctx.enter_context(nc.psum_tensor("PS", [P, 8, 512], F32))
        B_LOGIT, B_PT, B_Y = 4, 6, 7
        B_H1, B_H3, B_Y4 = 0, 2, 4

        scratch = nc.dram_tensor("bias_vectors", [HA + HB, VEC], F32, kind="Internal").ap()

        weights_in = [sem(f"weights_in{s}") for s in range(RING)]
        weights_used = sem("weights_used")
        wh_ready, wl_ready = sem("wh_ready"), sem("wl_ready")
        units_used = sem("units_used")
        hi_ready, lo_ready = sem("hi_ready"), sem("lo_ready")
        x_in = [sem("x_in0"), sem("x_in1")]
        x_back = sem("x_back")
        const_in = sem("const_in")
        table_in = sem("table_in")
        small_in = sem("small_in")
        vec_ready = sem("vec_ready")
        vec_out = sem("vec_out")
        bias_in = sem("bias_in")
        bias_masked = sem("bias_masked")
        sink_ready = sem("sink_ready")
        vec_ps = sem("vec_ps")
        xt_ps = sem("xt_ps")
        ev_act, ev_dve = sem("ev_act"), sem("ev_dve")
        va_ps, va_ready = sem("va_ps"), sem("va_ready")
        logits_ps = sem("logits_ps")
        dve_step = sem("dve_step")
        max_ready, exp_ready, rden_ready, probs_ready = sem("max_ready"), sem("exp_ready"), sem("rden_ready"), sem("probs_ready")
        pt_ps, pt_ready, y_ps, y_ready = sem("pt_ps"), sem("pt_ready"), sem("y_ps"), sem("y_ready")
        gate_sig, merged = sem("gate_sig"), sem("merged")
        p_in, p_ps = sem("p_in"), sem("p_ps")
        ln_in = sem("ln_in")
        ln2_in = sem("ln2_in")
        var_ready, std_ready, shift_ready = sem("var_ready"), sem("std_ready"), sem("shift_ready")
        scaled, gained = sem("scaled"), sem("gained")
        x1_pool, x1_dve = sem("x1_pool"), sem("x1_dve")
        rl_ps, rl_ready = sem("rl_ps"), sem("rl_ready")
        wr_hi, wr_lo = sem("wr_hi"), sem("wr_lo")
        ple_added = sem("ple_added")
        router_ps, rmax_ready, rexp_ready, mask_ready, pos_ps, routed = (
            sem("router_ps"), sem("rmax_ready"), sem("rexp_ready"), sem("mask_ready"), sem("pos_ps"), sem("routed"))
        sig_ready, acc_written = sem("sig_ready"), sem("acc_written")
        onehot_ready, gathered, xg_act, xg_dve = sem("onehot_ready"), sem("gathered"), sem("xg_act"), sem("xg_dve")
        silu_ready, h_ready, y_act, y_dve = sem("silu_ready"), sem("h_ready"), sem("y_act"), sem("y_dve")
        ht_ps, ht_act, ht_dve = sem("ht_ps"), sem("ht_act"), sem("ht_dve")
        spread_ready, ct_ps, ct_ready = sem("spread_ready"), sem("ct_ps"), sem("ct_ready")
        sum_ps = sem("sum_ps")
        out_pool, out_dve, out_done = sem("out_pool"), sem("out_dve"), sem("out_done")

        block = ctx.enter_context(nc.Block())

        PIECES1 = [(0, 0), (1, 0), (0, 1), (1, 1)]
        PIECES2 = [(0, 0), (0, 1), (1, 0), (1, 1)]

        def piece(r, t, h):
            return r[:, t, h * (D // 2):(h + 1) * (D // 2)]

        def FIRST(per, extra):
            return extra

        def later(i):
            return lambda per, extra: i * per + (per + extra)

        H_Y, H_M, H_P, H_X1 = 8, 12, 16, 17

        def slot(k):
            return ring[:, k % RING, :]

        def slot_kn(k, n):
            return slot(k).rearrange("q (k n) -> q k n", n=n)

        @block.sync
        def _(sp):
            def load(k, src, width):
                if k >= RING:
                    last, count = released[k - RING]
                    sp.wait_ge(last, count)
                sp.dma_start(slot_kn(k, width), src).then_inc(weights_in[k % RING], 16)

            released = [(wl_ready, 4 * (k + 1)) for k in range(K_MOE)]
            for u in range(UPS):
                released += [(weights_used, 2 * u + 1), (weights_used, 2 * u + 2)]
                if u >= PG_AHEAD:
                    released.append((wl_ready, 4 * (K_PG + u + 1)))
            released += [(weights_used, 2 * UPS + c + 1) for c in range(2 * W1C)]

            def rows(w, k0, nk, c0, width):
                return w[k0 * P:(k0 + nk) * P, c0:c0 + width].rearrange("(k p) n -> p k n", p=P)

            for h in range(2):
                c = slice(h * (D // 2), (h + 1) * (D // 2))
                for t in range(TT):
                    sp.dma_start(X[:, t, c], x[0, t * P:(t + 1) * P, c]).then_inc(x_in[h], 16)
            for c in range(N_KVA):
                load(K_KVA + c, rows(w_in[0], 8 * c, 8, C_KA, 2 * KVA * HD), 2 * KVA * HD)
            k = K_Q
            for c0 in (C_QA, C_QA + PANEL, C_QB, C_QB + PANEL, C_KB, C_KB + PANEL, C_VB, C_VB + PANEL,
                       *(C_GA + PANEL * j for j in range(2 * NP_))):
                for q in range(4):
                    load(k, rows(w_in[0], 4 * q, 4, c0, PANEL), PANEL)
                    k += 1
            for j in range(NP_):
                for w in (w_pa, w_pb):
                    for q in range(2):
                        load(k, rows(w[0], 4 * q, 4, PANEL * j, PANEL), PANEL)
                        k += 1
            for j in range(NP_):
                for q in range(4):
                    load(k, rows(w_o[0], 4 * q, 4, PANEL * j, PANEL), PANEL)
                    k += 1
            for c in range(N_PLE):
                load(k, rows(w_ple[0], 0, 2, 1024 * c, 1024), 1024)
                k += 1

            def ple_gate_load(k, n):
                load(k, rows(w_ple_gate[0], 4 * (n % 4), 4, PANEL * (n // 4), PANEL), PANEL)

            def expert_chunk(pair, c):
                m, q, e = c // (2 * W1C), c // 2 % W1C, c % 2
                expert = bass.ds(pair * 2 + e, 1)
                if m < 2:
                    return (w1, w3)[m][0][expert, 2 * P * q:2 * P * (q + 1), :].rearrange("e (k p) n -> p (e k) n", p=P), FF
                return w2[0][expert, P * q:P * (q + 1), :].rearrange("e (k p) n -> p (e k) n", p=P), D

            for n in range(PG_AHEAD):
                ple_gate_load(K_PG + n, n)
            k, n = K_MOE, PG_AHEAD
            for c in range(PAIR):
                load(k, *expert_chunk(0, c))
                k += 1
                if c % 2 == 1 and PG_AHEAD <= c // 2 < UPS:
                    ple_gate_load(k, n)
                    k, n = k + 1, n + 1
            assert k == K_LOOP and n == N_PG

            def pair_loads(pair, i):
                for c in range(PAIR):
                    src, width = expert_chunk(pair, c)
                    sp.wait_ge(weights_used, i * PAIR + (PAIR + c - RING + 1))
                    sp.dma_start(slot_kn(K_LOOP + c, width), src).then_inc(weights_in[(K_LOOP + c) % RING], 16)

            with sp.Fori(0, NPAIR - 1) as i:
                pair_loads(i + 1, i)
            sp.wait_ge(routed, 1)
            n_more = sp.value_load(n_more_t[0:1, 0:1], min_val=NPAIR - 1, max_val=NPAIR * MAXPASS - 1)
            with sp.If(n_more > NPAIR - 1):
                with sp.Fori(NPAIR - 1, n_more, NPAIR) as i:
                    with sp.Fori(0, NPAIR) as pair:
                        pair_loads(pair, i + pair)

        @block.gpsimd
        def _(pool):
            pool.wait_ge(vec_ready, 2)
            pool.dma_start(scratch[0:HA, :], vecA).then_inc(vec_out, 16)
            pool.dma_start(scratch[HA:HA + HB, :], vecB).then_inc(vec_out, 16)
            pool.wait_ge(vec_out, 32)
            pool.wait_ge(xt_ps, 8)
            for g in range(4):
                band = bass.AP(tensor=scratch.tensor, offset=8 * g * VEC, ap=[[1, P], [VEC, 8], [1, SEQ]])
                pool.dma_start((biasA, biasB)[g // 2][:, 8 * (g % 2):8 * (g % 2) + 8, :], band).then_inc(bias_in, 16)
            pool.wait_ge(bias_in, 64)
            pool.memset(biasA[0:CHUNK, :, 3 * CHUNK:SEQ], NEG)
            pool.memset(biasA[CHUNK:P, :, P:SEQ], NEG)
            pool.memset(biasA[0:CHUNK, :, 0:CHUNK], NEG)
            pool.memset(biasB[0:CHUNK, :, 0:CHUNK], NEG).then_inc(bias_masked, 1)

            for s in range(32):
                kt = s % 2 + 1
                pool.wait_ge(rden_ready, s + 1)
                for sub in range(2):
                    last = pool.tensor_scalar(S[:, s % 2, sub, 0:kt * P], S[:, s % 2, sub, 0:kt * P],
                                              rden[:, s % 2, sub:sub + 1], None, ALU.mult)
                last.then_inc(probs_ready, 1)

            def layer_norm_bias(r, n, pieces, b, done):
                for i in range(0, len(pieces), 2):
                    t, h = pieces[i]
                    pool.wait_ge(gained, 4 * n + i + 1)
                    pool.tensor_tensor(piece(r, t, h), piece(r, t, h), b[:, h * (D // 2):(h + 1) * (D // 2)], ALU.add).then_inc(done, 1)

            layer_norm_bias(X, 0, PIECES1, b1, x1_pool)
            for n in range(4 * K_PG + 4, 4 * K_MOE):
                pool.wait_ge(wh_ready, n + 1)
                pool.tensor_tensor(WL[:, n % UBUF, :], slot(n // 4)[:, UNIT * (n % 4):UNIT * (n % 4) + UNIT],
                                   WH[:, n % UBUF, :].bitcast(F32), ALU.subtract).then_inc(wl_ready, 1)
            layer_norm_bias(acc, 1, PIECES2, b2, out_pool)

        @block.scalar
        def _(act):
            act.dma_start(ident[:, :], square[:, 0:P]).then_inc(const_in, 16)
            act.dma_start(tri[:, :], square[:, P:2 * P]).then_inc(const_in, 16)
            act.dma_start(flip, square[:, 2 * P:3 * P]).then_inc(const_in, 16)
            act.dma_start(buckets, bucket[:, :]).then_inc(table_in, 16)
            act.dma_start(t5t, t5_table[:, :]).then_inc(table_in, 16)
            act.dma_start(relt[:, 0:2, :], relb_table[0, 0:2 * P, :].rearrange("(a p) h -> p a h", p=P)).then_inc(table_in, 16)
            act.dma_start(relt[0:REL_TABLE - 2 * P, 2, :], relb_table[0, 2 * P:REL_TABLE, :]).then_inc(table_in, 16)
            act.dma_start(sink[:, :], attn_sinks.partition_broadcast(P).rearrange("p a h -> p (a h)")).then_inc(small_in, 16)
            act.dma_start(brt[:, :], b_router.partition_broadcast(P)).then_inc(small_in, 16)

            def split_hi(d, q, k=None, body=None):
                k = d if k is None else k
                n = 4 * d + q
                more = 4 * LOOP_PANELS
                if q == 0:
                    count = 16 * (k // RING + 1)
                    act.wait_ge(weights_in[k % RING], count if body is None else body * (16 * more // RING) + count)
                if n >= UBUF:
                    act.wait_ge(units_used, n - UBUF + 1 if body is None else body * (4 * more) + (n - UBUF + 1))
                act.copy(WH[:, n % UBUF, :], slot(k)[:, UNIT * q:UNIT * q + UNIT]).then_inc(wh_ready, 1)

            def split_chunk(d, body=None):
                for q in range(4):
                    split_hi(d, q, body=body)

            def transposed_hi(first, groups, banks):
                for g in groups:
                    act.wait_ge(xt_ps, first + g + 1)
                    act.copy(XH[:, 2 * g:2 * g + 2, :].rearrange("q a b -> q (a b)"), PS[:, g % banks, :]).then_inc(hi_ready, 1)

            transposed_hi(0, range(8), 8)
            for c in range(N_KVA + 1):
                split_chunk(K_KVA + c)

            act.wait_ge(units_used, 4 * K_Q)
            for kv in range(KVA):
                for half in range(2):
                    last = act.copy(KA[HD * half:HD * half + HD, kv, :], PS[HD * kv:HD * kv + HD, 2 * P_KVA, 0:SEQ])
                last.then_inc(ev_act, 1)

            with act.Fori(0, N_Q // (4 * LOOP_PANELS)) as body:
                for j in range(LOOP_PANELS):
                    for c in range(1, 5):
                        split_chunk(K_Q + 4 * j + c, body)
                    act.wait_ge(units_used, body * (16 * LOOP_PANELS) + 4 * (K_Q + 4 * j + 4))
                    bank = body * 2 if j % 2 == 0 else body * -2 + 2
                    act.copy(QKT[:, bass.ds(body * (4 * LOOP_PANELS) + 4 * j, 2), :].rearrange("q a b -> q (a b)"),
                             PS[:, bass.ds(bank, 1), :].rearrange("q a b -> q (a b)")).then_inc(ev_act, 1)
            for j in range(2):
                for c in range(1, 5):
                    split_chunk(K_V + 4 * j + c)
                act.wait_ge(units_used, 4 * (K_V + 4 * j + 4))
                act.copy(VB[:, 0, PANEL * j:PANEL * (j + 1)], PS[:, 2 * ((P_V + j) % 2), :]).then_inc(ev_act, 1)

            def exps(s):
                act.wait_ge(max_ready, s + 1)
                kt = s % 2 + 1
                for sub in range(2):
                    last = act.activation(S[:, s % 2, sub, 0:kt * P], S[:, s % 2, sub, 0:kt * P], ACT.Exp,
                                          bias=nmax[:, s % 2, sub:sub + 1], accum_out=esum[:, s % 2, sub:sub + 1])
                if s < 16:
                    last = act.activation(esink[:, s % 2, :], esink[:, s % 2, :], ACT.Exp)
                last.then_inc(exp_ready, 1)

            def pt_copy(s):
                act.wait_ge(pt_ps, s + 1)
                kt = s % 2 + 1
                act.copy(PT[:, s % 2, 0:2 * kt, :].rearrange("q a b -> q (a b)"),
                         PS[:, B_PT, 0:2 * kt * P]).then_inc(pt_ready, 1)

            def gate_copy(j):
                act.wait_ge(units_used, 4 * (K_G + 4 * j + 4))
                act.copy(gates[:, j // 4, 4 * (j % 4):4 * (j % 4) + 2, :].rearrange("q a b -> q (a b)"),
                         PS[:, 2 * ((P_G + j) % 2), :]).then_inc(ev_act, 1)

            def operand_hi(blocks, g):
                act.copy(XH[:, 4 * g:4 * g + 4, :].rearrange("q a b -> q (a b)"),
                         blocks[:, 4 * g:4 * g + 4, :].rearrange("q a b -> q (a b)")).then_inc(hi_ready, 1)

            for s in range(32):
                if s >= 1:
                    pt_copy(s - 1)
                exps(s)
                split_hi(K_G + s + 1, 0)
                if s % 4 == 0 and s >= 4:
                    gate_copy(s // 4 - 1)
                for q in range(1, 4):
                    split_hi(K_G + s + 1, q)
                if s == 16:
                    for t in range(TT):
                        act.dma_start(X[:, t, :], x[0, t * P:(t + 1) * P, :]).then_inc(x_back, 16)
                if s >= 30:
                    act.wait_ge(y_ready, 16)
                    act.wait_ge(units_used, 4 * (K_M - 33 + s))
                    operand_hi(QKT, s - 30)
            pt_copy(31)
            gate_copy(7)
            act.wait_ge(units_used, 4 * K_M)
            act.wait_ge(y_ready, 32)
            for g in range(2, 4):
                operand_hi(QKT, g)
            act.dma_start(g1, ln1_g.partition_broadcast(P).rearrange("p a d -> p (a d)")).then_inc(ln_in, 16)
            act.dma_start(b1, ln1_b.partition_broadcast(P).rearrange("p a d -> p (a d)")).then_inc(ln_in, 16)
            act.dma_start(pnat, p[0, 0].rearrange("(t q) c -> q t c", q=P)).then_inc(p_in, 16)
            act.dma_start(WR, w_router.rearrange("(k p) e -> p k e", p=P)).then_inc(p_in, 16)
            act.dma_start(slots, square[:, 3 * P:]).then_inc(p_in, 16)

            act.wait_ge(ev_dve, P_M)
            act.wait_ge(ev_act, P_M)
            for n in range(2 * NP_):
                g = gates[:, n % 2, 4 * (n // 2):4 * (n // 2) + 4, :].rearrange("q a b -> q (a b)")
                act.activation(g, g, ACT.Sigmoid).then_inc(gate_sig, 1)
                split_chunk(K_M + 2 * n + 1)
                if n == 2 * NP_ - 1:
                    act.wait_ge(units_used, 4 * (K_O - 2))
                    for g in range(2):
                        act.wait_ge(merged, g + 1)
                        operand_hi(gates[:, 0, :, :], g)
                split_chunk(K_M + 2 * n + 2)
            act.wait_ge(units_used, 4 * K_O)
            for g in range(2, 4):
                act.wait_ge(merged, g + 1)
                operand_hi(gates[:, 0, :, :], g)
            for c in range(1, N_O + 1):
                split_chunk(K_O + c)
                if c == 4:
                    act.wait_ge(p_in, 48)
                    act.copy(WR2[:, :, 0, :], WR).then_inc(wr_hi, 1)
            act.wait_ge(p_ps, 1)
            act.wait_ge(units_used, 4 * K_PLE)
            act.copy(XH[:, KT - 2:, :].rearrange("q a b -> q (a b)"), PS[:, B_PT, :]).then_inc(hi_ready, 1)


            def layer_norm_scale(r, n, pieces, between=None):
                if between is not None:
                    between(-2)
                act.wait_ge(var_ready, n + 1)
                act.activation(rstd[:, :], mv[:, :, 1], ACT.Sqrt, bias=epst[:, 0:1]).then_inc(std_ready, 1)
                if between is not None:
                    between(-1)
                act.wait_ge(shift_ready, n + 1)
                for i, (t, h) in enumerate(pieces):
                    act.activation(piece(r, t, h), piece(r, t, h), ACT.Identity, bias=shift[:, t:t + 1],
                                   scale=rstd[:, t:t + 1]).then_inc(scaled, 1)
                    if between is not None:
                        between(i)

            def ple_split(i):
                for q in {-2: (0,), -1: (1,), 2: (2, 3)}.get(i, ()):
                    split_hi(K_PLE + 1, q)

            def ple_copy(n):
                act.wait_ge(units_used, 4 * (K_PLE + n // 2 + 1))
                act.copy(ple[:, :, PANEL * n:PANEL * n + PANEL], PS[:, 2 * n:2 * n + 2, :]).then_inc(ev_act, 1)

            layer_norm_scale(X, 0, PIECES1, ple_split)
            ple_copy(0)
            ple_copy(1)
            transposed_hi(8, range(2), 4)
            ple_copy(2)
            transposed_hi(8, range(2, 4), 4)
            ple_copy(3)
            transposed_hi(8, range(4, 8), 4)
            split_chunk(K_PG)
            act.wait_ge(x1_pool, 2)
            act.wait_ge(x1_dve, 2)
            act.dma_start(g2, ln2_g.partition_broadcast(P).rearrange("p a d -> p (a d)")).then_inc(ln2_in, 16)
            act.dma_start(b2, ln2_b.partition_broadcast(P).rearrange("p a d -> p (a d)")).then_inc(ln2_in, 16)

            act.wait_ge(rmax_ready, 1)
            for t in range(TT):
                last = act.activation(r_ex[:, NE * t:NE * t + NE], r_rank[:, NE * t:NE * t + NE], ACT.Exp,
                                      bias=r_m[:, t:t + 1], accum_out=r_s[:, t:t + 1])
            last.then_inc(rexp_ready, 1)

            for j in range(NP_):
                act.mul(acc[:, :, PANEL * j:PANEL * j + PANEL], X[:, :, PANEL * j:PANEL * j + PANEL], ALPHA).then_inc(acc_written, 1)

            def ple_gate(n):
                act.wait_ge(units_used, 4 * (K_PG + 4 * n + 4))
                if n >= 1:
                    act.wait_ge(ple_added, n)
                b = B_Y4 + 2 * ((n + 1) % 2)
                act.activation(sig, PS[:, b:b + 2, :], ACT.Sigmoid).then_inc(sig_ready, 1)

            for c in range(1, PG_AHEAD):
                split_chunk(K_PG + c)
            act.wait_ge(routed, 1)
            n_more = act.value_load(n_more_t[0:1, 0:1], min_val=NPAIR - 1, max_val=NPAIR * MAXPASS - 1)

            def gathered_copy(it, ahead):
                act.wait_ge(gathered, it(2, 2 * ahead + 1))
                act.copy(XG[:, 0:8, :].rearrange("q k s -> q (k s)"),
                         PS[:, 0:2, :].rearrange("q a b -> q (a b)")).then_inc(xg_act, 1)

            def ct_copy(it):
                act.wait_ge(ct_ps, it(1, 1))
                act.copy(CT, PS[:, B_H1, 0:SEQ]).then_inc(ct_ready, 1)

            gathered_copy(FIRST, 0)

            def pair_steps(it):
                if it is FIRST:
                    for u in range(PG_AHEAD, 9):
                        for q in range(4):
                            split_hi(K_PG + u, q, K_MOE + first_at(u) + 2)
                        if u == 4:
                            ple_gate(0)
                    ple_gate(1)
                for f in range(2):
                    act.wait_ge(weights_used, it(PAIR, 2 * W1C))
                    act.activation(HS[:, PANEL * f:PANEL * f + PANEL], PS[:, B_H1 + f, :], ACT.Silu).then_inc(silu_ready, 1)
                if it is FIRST:
                    for u in range(9, 16):
                        for q in range(4):
                            split_hi(K_PG + u, q, K_MOE + first_at(u) + 2)
                        if u == 12:
                            ple_gate(2)
                    ple_gate(3)
                act.wait_ge(ht_ps, it(2, 1))
                act.copy(HT[:, 0:4, :].rearrange("q k s -> q (k s)"), PS[:, B_H1, :]).then_inc(ht_act, 1)
                gathered_copy(it, 1)
                ct_copy(it)
                act.wait_ge(weights_used, it(PAIR, PAIR))
                act.copy(Y[:, 0:2 * PANEL], PS[:, B_Y4:B_Y4 + 2, :].rearrange("q a b -> q (a b)")).then_inc(y_act, 1)

            pair_steps(FIRST)
            with act.Fori(0, n_more) as i:
                pair_steps(later(i))

            layer_norm_scale(acc, 1, PIECES2)
            for i, (t, h) in enumerate(PIECES2):
                act.wait_ge((out_pool, out_dve)[i % 2], i // 2 + 1)
                act.dma_start(out[0, t * P:(t + 1) * P, h * (D // 2):(h + 1) * (D // 2)], piece(acc, t, h)).then_inc(out_done, 16)
            act.wait_ge(out_done, 16 * len(PIECES2))

        @block.tensor
        def _(pe):
            def arrived(k, more=0):
                pe.wait_ge(weights_in[k % RING], more * 16 + 16 * (k // RING + 1))

            def bank_pair(n):
                return PS[:, 2 * (n % 2):2 * (n % 2) + 2, :]

            def unit(n, more=0):
                pe.wait_ge(wl_ready, more + (n + 1))

            def parts(lhs, rhs):
                return (lhs[0], rhs[0]), (lhs[0], rhs[1]), (lhs[1], rhs[0])

            def columns(d, ps, blocks, first, last, more=0):
                o = ps.rearrange("q a (b t) -> q (a b) t", t=SEQ)
                for q in range(4):
                    n = 4 * d + q
                    unit(n, more)
                    for m in range(4):
                        w = [W[:, n % UBUF, P * m:P * m + P] for W in (WH, WL)]
                        x_ = [A[:, blocks + q, :] for A in (XH, XL)]
                        for i, (a, b) in enumerate(parts(w, x_)):
                            mm = pe.matmul(o[:, m, :], a, b, start=(first and q == 0 and m % 2 == 0 and i == 0),
                                           stop=(last and q == 3 and i == 2), skip_group_check=True)
                    mm.then_inc(units_used, 1)

            def tokens(d, ps, blocks, first, last, more=0):
                for q in range(4):
                    n = 4 * d + q
                    unit(n, more)
                    for t in range(TT):
                        w = [W[:, n % UBUF, :] for W in (WH, WL)]
                        x_ = [A[:, blocks + q, P * t:P * t + P] for A in (XH, XL)]
                        for i, (a, b) in enumerate(parts(x_, w)):
                            mm = pe.matmul(ps[:, t, :], a, b, start=(first and q == 0 and i == 0),
                                           stop=(last and q == 3 and i == 2), skip_group_check=True)
                    mm.then_inc(units_used, 1)

            def transpose_x(groups, banks):
                for g in groups:
                    for b in range(4):
                        k, t = 2 * g + b // 2, b % 2
                        mm = pe.transpose(PS[:, g % banks, P * b:P * b + P], X[:, t, P * k:P * k + P], ident[:, :])
                    mm.then_inc(xt_ps, 1)

            pe.wait_ge(const_in, 48)
            for half in range(2):
                pe.wait_ge(x_in[half], 16 * TT)
                transpose_x(range(4 * half, 4 * half + 4), 8)
            pe.wait_ge(lo_ready, H_Y)

            for n in range(4 * K_KVA, 4 * K_Q):
                unit(n)
                for h in range(2):
                    k = 2 * n + h
                    for v in range(2):
                        c = UNIT // 2 * h + P * v
                        for i, (a, b) in enumerate(parts([W[:, n % UBUF, c:c + P] for W in (WH, WL)], [A[:, k, :] for A in (XH, XL)])):
                            mm = pe.matmul(PS[:, 2 * P_KVA + v, 0:SEQ], a, b, start=(k == 0 and i == 0), stop=(k == KT - 1 and i == 2))
                mm.then_inc(units_used, 1)
            pe.wait_ge(table_in, 64)
            pe.matmul(PS[0:HA, B_LOGIT, 0:VEC], t5t, buckets, start=True, stop=True)
            for a in range(3):
                n = min(P, REL_TABLE - P * a)
                mm = pe.matmul(PS[0:HB, B_LOGIT + 1, P * (3 - a) - n:P * (3 - a)], relt[0:n, a, :], flip[0:n, P - n:P],
                               start=True, stop=True)
            mm.then_inc(vec_ps, 1)

            with pe.Fori(0, N_Q // 8) as body:
                for j in range(2):
                    pe.wait_ge(ev_act, body * 2 + (P_Q + j - 1))
                    pe.wait_ge(ev_dve, body * 2 + (P_Q + j - 1))
                    for c in range(4):
                        columns(K_Q + 4 * j + c, bank_pair(P_Q + j), 4 * c, c == 0, c == 3, body * 32)
            for j in range(2):
                pe.wait_ge(ev_act, P_V + j - 1)
                pe.wait_ge(ev_dve, P_V + j - 1)
                for c in range(4):
                    tokens(K_V + 4 * j + c, bank_pair(P_V + j), 4 * c, c == 0, c == 3)

            def logits(s):
                br, i, t = s // 16, s % 16 // 2, s % 2
                keys = P * (t + 1)
                pe.wait_ge(max_ready, s)
                for sub in range(2):
                    h = slice(HD * sub, HD * sub + HD)
                    rhs = KA[h, i // 4, 0:keys] if br == 0 else QKT[h, 16 + i, 0:keys]
                    mm = pe.matmul(PS[:, B_LOGIT + sub, 0:keys], QKT[h, 8 * br + i, P * t:P * t + P],
                                   rhs, start=True, stop=True)
                mm.then_inc(logits_ps, 1)

            def transposes(s):
                t = s % 2
                pe.wait_ge(probs_ready, s + 1)
                pe.wait_ge(pt_ready, s)
                for sub in range(2):
                    for k in range(t + 1):
                        n = sub * (t + 1) + k
                        mm = pe.transpose(PS[:, B_PT, P * n:P * n + P], S[:, s % 2, sub, P * k:P * k + P], ident[:, :])
                mm.then_inc(pt_ps, 1)

            def values(s):
                br, i, t = s // 16, s % 16 // 2, s % 2
                pe.wait_ge(pt_ready, s + 1)
                pe.wait_ge(y_ready, s)
                for k in range(t + 1):
                    for sub in range(2):
                        v = VA[:, k, HD * (i // 4):HD * (i // 4) + HD] if br == 0 else VB[:, k, HD * (2 * i + sub):HD * (2 * i + sub + 1)]
                        mm = pe.matmul(PS[HD * sub:HD * sub + HD, B_Y, 0:P], v, PT[:, s % 2, sub * (t + 1) + k, :],
                                       start=(k == 0), stop=(k == t), skip_group_check=True)
                mm.then_inc(y_ps, 1)

            for t in range(TT):
                mm = pe.transpose(PS[:, B_PT, P * t:P * t + P], VAT[:, P * t:P * t + P], ident[:, :])
            mm.then_inc(va_ps, 1)

            pe.wait_ge(bias_masked, 1)
            pe.wait_ge(ev_act, P_G - 1)
            pe.wait_ge(ev_dve, P_G - 1)
            for s in range(34):
                if s == 1:
                    pe.wait_ge(ev_act, P_G)
                    pe.wait_ge(ev_dve, P_G)
                    pe.wait_ge(va_ready, 1)
                if s < 32:
                    logits(s)
                if 1 <= s <= 32:
                    transposes(s - 1)
                if 2 <= s:
                    values(s - 2)
                if s < 32:
                    j, c = s // 4, s % 4
                    if c == 0:
                        pe.wait_ge(ev_act, P_G + j - 1)
                        pe.wait_ge(ev_dve, P_G + j - 1)
                    columns(K_G + s, bank_pair(P_G + j), 4 * c, c == 0, c == 3)

            pe.wait_ge(ev_act, P_M)
            with pe.Fori(0, N_M // 8) as body:
                for n in range(4):
                    pe.wait_ge(ev_dve, body * 4 + (P_M + n - 1))
                    for c in range(2):
                        pe.wait_ge(lo_ready, H_Y + 2 * (n % 2) + c + 1)
                        columns(K_M + 2 * n + c, bank_pair(P_M + n), 8 * (n % 2) + 4 * c, c == 0, c == 1, body * 32)

            pe.wait_ge(p_in, 48)
            for k in range(2):
                for t in range(TT):
                    mm = pe.transpose(PS[:, B_PT, P * (2 * k + t):P * (2 * k + t) + P], pnat[:, t, P * k:P * k + P], ident[:, :])
            mm.then_inc(p_ps, 1)

            with pe.Fori(0, N_O // 8) as body:
                for j in range(2):
                    pe.wait_ge(ev_dve, body * 2 + (P_O + j - 1))
                    for c in range(4):
                        pe.wait_ge(lo_ready, H_M + c + 1)
                        tokens(K_O + 4 * j + c, bank_pair(P_O + j), 4 * c, c == 0, c == 3, body * 32)

            pe.wait_ge(lo_ready, H_X1)
            for c in range(N_PLE):
                for q in range(4):
                    n = 4 * (K_PLE + c) + q
                    k, b = q // 2, 4 * c + 2 * (q % 2)
                    if c == 0 and q < 2:
                        pe.wait_ge(ev_dve, P_PLE - 1 + q)
                    unit(n)
                    for t in range(TT):
                        w = [W[:, n % UBUF, :] for W in (WH, WL)]
                        x_ = [A[:, KT - 2 + k, P * t:P * t + P] for A in (XH, XL)]
                        for i, (a, m) in enumerate(parts(x_, w)):
                            mm = pe.matmul(PS[:, b + t, :], a, m, start=(k == 0 and i == 0), stop=(k == 1 and i == 2),
                                           skip_group_check=True)
                    mm.then_inc(units_used, 1)

            def router(g):
                pe.wait_ge(lo_ready, H_X1 + g + 1)
                for k in range(2 * g, 2 * g + 2):
                    pe.matmul(PS[0:2 * NE, B_LOGIT, 0:SEQ], WR2[:, k, :, :].rearrange("q a e -> q (a e)"), XH[:, k, :],
                              start=(k == 0), stop=False, skip_group_check=True)
                    mm = pe.matmul(PS[0:NE, B_LOGIT, 0:SEQ], WR2[:, k, 0, :], XL[:, k, :],
                                   start=False, stop=(k == KT - 1), skip_group_check=True)
                return mm

            pe.wait_ge(ev_act, P_M + 2)
            for g in range(8):
                if g % 4 == 0:
                    pe.wait_ge(x1_pool, g // 4 + 1)
                    pe.wait_ge(x1_dve, g // 4 + 1)
                if g >= 4:
                    pe.wait_ge(lo_ready, H_X1 + g - 3)
                transpose_x([g], 4)
                if g == 2:
                    pe.wait_ge(wr_lo, 1)
                    pe.wait_ge(ev_act, P_M + 3)
                if g >= 2:
                    router(g - 2)
            router(6)
            mm = router(7)
            mm.then_inc(rl_ps, 1)
            pe.wait_ge(rl_ready, 1)
            for t in range(TT):
                mm = pe.transpose(PS[:, B_LOGIT, SEQ + 2 * NE * t:SEQ + 2 * NE * (t + 1)], RL[:, P * t:P * t + P], ident[0:2 * NE, 0:2 * NE])
            mm.then_inc(router_ps, 1)

            def positions():
                pe.wait_ge(mask_ready, 1)
                m = r_mask.rearrange("q (t e) -> q t e", t=TT)
                o = PS[:, B_LOGIT + 1, 0:3 * NE].rearrange("q (t e) -> q t e", e=NE)
                pe.matmul(o[:, 0, :], tri[:, :], m[:, 0, :], start=True, stop=True)
                pe.matmul(o[:, 1, :], ones, m[:, 0, :], start=True, stop=False)
                pe.matmul(o[:, 1, :], tri[:, :], m[:, 1, :], start=False, stop=True)
                pe.matmul(o[:, 2, :], ones, m[:, 0, :], start=True, stop=False)
                pe.matmul(o[:, 2, :], ones, m[:, 1, :], start=False, stop=True).then_inc(pos_ps, 1)

            def ple_gate(n):
                b = B_Y4 + 2 * ((n // 4 + 1) % 2)
                if n % 4 == 0 and n >= 8:
                    pe.wait_ge(sig_ready, n // 4 - 1)
                tokens(K_PG + n, PS[:, b:b + 2, :], 4 * (n % 4), n % 4 == 0, n % 4 == 3)

            pe.wait_ge(ev_act, P_M + NP_)
            for n in range(PG_AHEAD):
                ple_gate(n)
            positions()

            def gather(it, ahead):
                pe.wait_ge(onehot_ready, it(1, ahead + 1))
                o = PS[:, 0:4, :].rearrange("q a (k s) -> q (a k) s", s=2 * SLOTS)
                for k in range(KT):
                    for t in range(TT):
                        mm = pe.matmul(o[:, k, :], X[:, t, P * k:P * k + P], OH[:, t, :, :].rearrange("q e s -> q (e s)"),
                                       start=(k % 4 == 0 and t == 0), stop=(t == TT - 1), skip_group_check=True)
                    if k % 8 == 7:
                        mm.then_inc(gathered, 1)

            def pair_slot(it, first, later):
                return K_MOE + first if it is FIRST else K_LOOP + later

            def pair_arrived(it, first, later):
                k = pair_slot(it, first, later)
                if it is FIRST:
                    arrived(k)
                else:
                    pe.wait_ge(weights_in[k % RING], it(PAIR // RING * 16, 16 * (k // RING + 1 - PAIR // RING)))

            def up(it, m, c):
                for e in range(2):
                    pair_arrived(it, first_at(W1C * m + c) + e, 2 * (W1C * m + c) + e)
                for q in range(2):
                    for f in range(2):
                        for e in range(2):
                            k = pair_slot(it, first_at(W1C * m + c) + e, 2 * (W1C * m + c) + e)
                            mm = pe.matmul(PS[SLOTS * e:SLOTS * e + SLOTS, (B_H1, B_H3)[m] + f, :],
                                           XG[:, 2 * c + q, SLOTS * e:SLOTS * e + SLOTS],
                                           slot_kn(k, FF)[:, q, PANEL * f:PANEL * f + PANEL],
                                           start=(c == 0 and q == 0), stop=(c == W1C - 1 and q == 1), skip_group_check=True)
                mm.then_inc(weights_used, 2)

            def down(it, c):
                for e in range(2):
                    pair_arrived(it, first_at(UPS) + 2 * c + e, 2 * UPS + 2 * c + e)
                for j in range(NP_):
                    for e in range(2):
                        k = pair_slot(it, first_at(UPS) + 2 * c + e, 2 * UPS + 2 * c + e)
                        mm = pe.matmul(PS[SLOTS * e:SLOTS * e + SLOTS, B_Y4 + j, :], HT[:, c, SLOTS * e:SLOTS * e + SLOTS],
                                       slot(k)[:, PANEL * j:PANEL * j + PANEL],
                                       start=(c == 0), stop=(c == W1C - 1), skip_group_check=True)
                mm.then_inc(weights_used, 2)

            def turn_hidden(it):
                for f in range(2):
                    pe.wait_ge(h_ready, it(2, f + 1))
                    for b in range(4):
                        mm = pe.transpose(PS[:, B_H1 + f, P * b:P * b + P], HS[:, PANEL * f + P * b:PANEL * f + P * b + P], ident[:, :])
                    mm.then_inc(ht_ps, 1)

            def spread_matrix(it):
                pe.wait_ge(spread_ready, it(1, 1))
                pe.wait_ge(xg_act, it(1, 2))
                for t in range(TT):
                    mm = pe.transpose(PS[:, B_H1, P * t:P * t + P], OHW[:, t, :, :].rearrange("q e s -> q (e s)"), ident[:, :])
                mm.then_inc(ct_ps, 1)

            def spread(it, n):
                if n % 2 == 0 and n < 4:
                    pe.wait_ge((y_act, y_dve)[n // 2], it(1, 0))
                if n >= 4:
                    pe.wait_ge(acc_written, it(8, NP_ - 8 + n - 3))
                pe.matmul(PS[:, B_Y4 + n % 4, :], CT[:, P * (n // 4):P * (n // 4) + P], Y[:, PANEL * (n % 4):PANEL * (n % 4) + PANEL],
                          start=True, stop=True).then_inc(sum_ps, 1)

            gather(FIRST, 0)
            pe.wait_ge(routed, 1)
            n_more = pe.value_load(n_more_t[0:1, 0:1], min_val=NPAIR - 1, max_val=NPAIR * MAXPASS - 1)

            def pair_steps(it):
                first = it is FIRST
                if not first:
                    pe.wait_ge(ct_ready, it(1, 0))
                pe.wait_ge(xg_act, it(1, 1))
                for u in range(UPS):
                    if u == 4:
                        pe.wait_ge(xg_dve, it(1, 1))
                    up(it, u // W1C, u % W1C)
                    if first and u >= PG_AHEAD:
                        ple_gate(u)
                    if not first and u < 8:
                        spread(it, u)
                turn_hidden(it)
                pe.wait_ge(ht_act, it(1, 1))
                pe.wait_ge(ht_dve, it(1, 1))
                if first:
                    pe.wait_ge(sig_ready, NP_)
                else:
                    pe.wait_ge(acc_written, it(8, NP_))
                for c in range(W1C):
                    down(it, c)
                    if c == 0:
                        gather(it, 1)
                    if c == 3:
                        spread_matrix(it)

            pair_steps(FIRST)
            with pe.Fori(0, n_more) as i:
                pair_steps(later(i))
            last = later(n_more)
            pe.wait_ge(ct_ready, last(1, 0))
            for n in range(8):
                spread(last, n)

        @block.vector
        def _(dve):
            steps = [0]

            def link(ins, base=0):
                steps[0] += 1
                ins.then_inc(dve_step, 1)
                dve.wait_ge(dve_step, base + steps[0])

            def bank2(n, b):
                return PS[:, 2 * (n % 2) + b, :]

            dve.memset(epst[:, :], LN_EPS)
            dve.memset(vecB[:, 0:VEC - REL_TABLE], 0.0)

            def split_lo(d, q, k=None, body=None):
                k = d if k is None else k
                n = 4 * d + q
                dve.wait_ge(wh_ready, n + 1 if body is None else body * (16 * LOOP_PANELS) + (n + 1))
                dve.tensor_tensor(WL[:, n % UBUF, :], slot(k)[:, UNIT * q:UNIT * q + UNIT],
                                  WH[:, n % UBUF, :].bitcast(F32), ALU.subtract).then_inc(wl_ready, 1)

            def split_chunk(d, body=None):
                for q in range(4):
                    split_lo(d, q, body=body)

            def transposed_lo(first, groups, banks):
                for g in groups:
                    dve.wait_ge(hi_ready, first + g + 1)
                    c = slice(2 * g, 2 * g + 2)
                    dve.tensor_tensor(XL[:, c, :].rearrange("q a b -> q (a b)"), PS[:, g % banks, :],
                                      XH[:, c, :].rearrange("q a b -> q (a b)").bitcast(F32), ALU.subtract).then_inc(lo_ready, 1)

            transposed_lo(0, range(8), 8)
            for c in range(N_KVA + 1):
                split_chunk(K_KVA + c)
            dve.wait_ge(vec_ps, 1)
            dve.tensor_copy(vecA, PS[0:HA, B_LOGIT, 0:VEC]).then_inc(vec_ready, 1)
            dve.tensor_copy(vecB[:, VEC - REL_TABLE:VEC], PS[0:HB, B_LOGIT + 1, VEC - REL_TABLE:VEC]).then_inc(vec_ready, 1)
            dve.wait_ge(small_in, 32)
            dve.tensor_scalar(nsink[:, :], sink[:, :], -1.0, None, ALU.mult).then_inc(sink_ready, 1)
            dve.wait_ge(units_used, 4 * K_Q)
            dve.tensor_copy(VAT, PS[:, 2 * P_KVA + 1, 0:SEQ]).then_inc(ev_dve, 2)
            with dve.Fori(0, N_Q // (4 * LOOP_PANELS)) as body:
                for j in range(LOOP_PANELS):
                    for c in range(1, 5):
                        split_chunk(K_Q + 4 * j + c, body)
                    dve.wait_ge(units_used, body * (16 * LOOP_PANELS) + 4 * (K_Q + 4 * j + 4))
                    bank = body * 2 + 1 if j % 2 == 0 else body * -2 + 3
                    dve.tensor_copy(QKT[:, bass.ds(body * (4 * LOOP_PANELS) + 4 * j + 2, 2), :].rearrange("q a b -> q (a b)"),
                                    PS[:, bass.ds(bank, 1), :].rearrange("q a b -> q (a b)")).then_inc(ev_dve, 1)
            for j in range(2):
                for c in range(1, 5):
                    split_chunk(K_V + 4 * j + c)
                dve.wait_ge(units_used, 4 * (K_V + 4 * j + 4))
                dve.tensor_copy(VB[:, 1, PANEL * j:PANEL * (j + 1)], bank2(P_V + j, 1)).then_inc(ev_dve, 1)

            dve.wait_ge(va_ps, 1)
            dve.tensor_copy(VA[:, :, :].rearrange("q t d -> q (t d)"), PS[:, B_PT, 0:TT * P]).then_inc(va_ready, 1)
            dve.wait_ge(bias_masked, 1)
            dve.wait_ge(sink_ready, 1)

            def biased(s):
                br, i, t = s // 16, s % 16 // 2, s % 2
                keys, b = P * (t + 1), s % 2
                dve.wait_ge(logits_ps, s + 1)
                if s >= 2:
                    dve.wait_ge(pt_ps, s - 1)
                ps = PS[:, B_LOGIT:B_LOGIT + 2, 0:keys]
                bias, h0 = (biasA, biasB)[br], 2 * i
                link(dve.scalar_tensor_tensor(out=S[:, b, :, 0:keys], in0=ps, scalar=SCALE,
                                              in1=bias[:, h0:h0 + 2, 0:keys][:, :, ::-1], op0=ALU.mult, op1=ALU.add))
                if br == 1:
                    dve.tensor_reduce(nmax[:, b, :], S[:, b, :, 0:keys], AX.X, ALU.max, negate=True).then_inc(max_ready, 1)
                else:
                    link(dve.tensor_reduce(nmax[:, b, :], S[:, b, :, 0:keys], AX.X, ALU.max, negate=True))
                    link(dve.tensor_tensor(nmax[:, b, :], nmax[:, b, :], nsink[:, 2 * i:2 * i + 2], ALU.min))
                    dve.tensor_tensor(esink[:, b, :], sink[:, 2 * i:2 * i + 2], nmax[:, b, :], ALU.add).then_inc(max_ready, 1)

            def denominators(s):
                b = s % 2
                dve.wait_ge(exp_ready, s + 1)
                if s < 16:
                    link(dve.tensor_tensor(esum[:, b, :], esum[:, b, :], esink[:, b, :], ALU.add))
                dve.reciprocal(rden[:, b, :], esum[:, b, :]).then_inc(rden_ready, 1)

            def outputs(s):
                br, i, t = s // 16, s % 16 // 2, s % 2
                dve.wait_ge(y_ps, s + 1)
                dve.tensor_copy(QKT[:, 8 * br + i, P * t:P * t + P], PS[:, B_Y, 0:P]).then_inc(y_ready, 1)

            def gate_copy(j):
                dve.wait_ge(units_used, 4 * (K_G + 4 * j + 4))
                dve.tensor_copy(gates[:, j // 4, 4 * (j % 4) + 2:4 * (j % 4) + 4, :].rearrange("q a b -> q (a b)"),
                                bank2(P_G + j, 1)).then_inc(ev_dve, 1)

            def operand_lo(blocks, first, g):
                dve.wait_ge(hi_ready, first + g + 1)
                c = slice(4 * g, 4 * g + 4)
                dve.tensor_tensor(XL[:, c, :].rearrange("q a b -> q (a b)"), blocks[:, c, :].rearrange("q a b -> q (a b)"),
                                  XH[:, c, :].rearrange("q a b -> q (a b)").bitcast(F32), ALU.subtract).then_inc(lo_ready, 1)

            for s in range(32):
                biased(s)
                if s >= 2:
                    outputs(s - 2)
                denominators(s)
                split_lo(K_G + s + 1, 0)
                if s % 4 == 0 and s >= 4:
                    gate_copy(s // 4 - 1)
                for q in range(1, 4):
                    split_lo(K_G + s + 1, q)
                if s >= 30:
                    operand_lo(QKT, H_Y, s - 30)
            gate_copy(7)
            outputs(30)
            outputs(31)

            for g in range(2, 4):
                operand_lo(QKT, H_Y, g)

            for n in range(2 * NP_):
                split_chunk(K_M + 2 * n + 1)
                if n == 2 * NP_ - 1:
                    for g in range(2):
                        operand_lo(gates[:, 0, :, :], H_M, g)
                split_chunk(K_M + 2 * n + 2)
                j, br = n // 2, n % 2
                g = gates[:, br, 4 * j:4 * j + 4, :].rearrange("q a b -> q (a b)")
                dve.wait_ge(gate_sig, n + 1)
                dve.wait_ge(units_used, 4 * (K_M + 2 * n + 2))
                b = 2 * ((P_M + n) % 2)
                dve.tensor_tensor(g, PS[:, b:b + 2, :].rearrange("q a b -> q (a b)"), g, ALU.mult).then_inc(ev_dve, 1)
                if br == 1:
                    dve.wait_ge(ev_dve, P_M + n + 1)
                    ga = gates[:, 0, 4 * j:4 * j + 4, :].rearrange("q a b -> q (a b)")
                    dve.tensor_tensor(ga, ga, g, ALU.add).then_inc(merged, 1)
            for g in range(2, 4):
                operand_lo(gates[:, 0, :, :], H_M, g)
            dve.wait_ge(x_back, 16 * TT)
            for j in range(NP_):
                for c in range(1, 5):
                    split_chunk(K_O + 4 * j + c)
                if j == 0:
                    dve.wait_ge(wr_hi, 1)
                    dve.tensor_tensor(WR2[:, :, 1, :], WR, WR2[:, :, 0, :].bitcast(F32), ALU.subtract).then_inc(wr_lo, 1)
                dve.wait_ge(units_used, 4 * (K_O + 4 * j + 4))
                if j == NP_ - 1:
                    dve.wait_ge(hi_ready, H_X1)
                    dve.tensor_tensor(XL[:, KT - 2:, :].rearrange("q a b -> q (a b)"), PS[:, B_PT, :],
                                      XH[:, KT - 2:, :].rearrange("q a b -> q (a b)").bitcast(F32), ALU.subtract).then_inc(lo_ready, 1)
                xs = X[:, :, PANEL * j:PANEL * j + PANEL]
                dve.scalar_tensor_tensor(out=xs, in0=xs, scalar=ALPHA,
                                         in1=PS[:, 2 * ((P_O + j) % 2):2 * ((P_O + j) % 2) + 2, :],
                                         op0=ALU.mult, op1=ALU.add).then_inc(ev_dve, 1)
                dve.wait_ge(ev_dve, P_O + j + 1)
                for t in range(TT):
                    last = dve.bn_stats(stats[:, t, j, :], X[:, t, PANEL * j:PANEL * j + PANEL])
            link(last)

            def layer_norm_gain(r, n, pieces, g, vectors, b, done, between=None):
                for t in range(TT):
                    last = dve.bn_aggr(mv[:, t, :], stats[:, t, :, :].rearrange("q a b -> q (a b)"))
                last.then_inc(var_ready, 1)
                if between is not None:
                    between(-2)
                dve.wait_ge(std_ready, n + 1)
                link(dve.reciprocal(rstd[:, :], rstd[:, :]))
                dve.scalar_tensor_tensor(out=shift[:, :], in0=mv[:, :, 0], scalar=-1.0, in1=rstd[:, :],
                                         op0=ALU.mult, op1=ALU.mult).then_inc(shift_ready, 1)
                if between is not None:
                    between(-1)
                dve.wait_ge(vectors, 32)
                for i, (t, h) in enumerate(pieces):
                    dve.wait_ge(scaled, 4 * n + i + 1)
                    dve.tensor_tensor(piece(r, t, h), piece(r, t, h), g[:, h * (D // 2):(h + 1) * (D // 2)], ALU.mult).then_inc(gained, 1)
                    if i % 2 == 1:
                        dve.wait_ge(gained, 4 * n + i + 1)
                        dve.tensor_tensor(piece(r, t, h), piece(r, t, h), b[:, h * (D // 2):(h + 1) * (D // 2)], ALU.add).then_inc(done, 1)
                    if between is not None:
                        between(i)


            def ple_split(i):
                for q in {-2: (0,), -1: (1,), 2: (2, 3)}.get(i, ()):
                    split_lo(K_PLE + 1, q)

            layer_norm_gain(X, 0, PIECES1, g1, ln_in, b1, x1_dve, ple_split)
            dve.memset(ones, 1.0)
            transposed_lo(H_X1, range(8), 4)
            split_chunk(K_PG)
            dve.wait_ge(rl_ps, 1)
            dve.tensor_copy(RL, PS[0:2 * NE, B_LOGIT, 0:SEQ]).then_inc(rl_ready, 1)

            def te(a):
                return a.rearrange("q (t e) -> q t e", t=TT)

            def tge(a):
                return a.rearrange("q (t e) -> q t e", e=EPG)

            def rank(val, r, g, n):
                for i in range(n):
                    last = dve.memset(r[:, :, i], float(n - 1 - i))
                link(last)
                for s in range(1, n):
                    link(dve.tensor_tensor(g[:, :, 0:n - s], val[:, :, 0:n - s], val[:, :, s:n], ALU.is_ge))
                    link(dve.tensor_tensor(r[:, :, s:n], r[:, :, s:n], g[:, :, 0:n - s], ALU.add))
                    link(dve.tensor_tensor(r[:, :, 0:n - s], r[:, :, 0:n - s], g[:, :, 0:n - s], ALU.subtract))

            def onehots(it2):
                for e in range(2):
                    for t in range(TT):
                        last = dve.tensor_scalar(OH[:, t, e, :], slots, posm[:, t, bass.ds(it2 + e, 1)], None, ALU.is_equal)
                last.then_inc(onehot_ready, 1)

            def route():
                dve.wait_ge(router_ps, 1)
                link(dve.tensor_reduce(te(r_rank), PS[:, B_LOGIT, SEQ:SEQ + 2 * TT * NE].rearrange("q (t a e) -> q t e a", t=TT, e=NE),
                                       AX.X, ALU.add))
                dve.tensor_reduce(r_m, te(r_rank), AX.X, ALU.max, negate=True).then_inc(rmax_ready, 1)
                dve.wait_ge(rexp_ready, 1)
                link(dve.reciprocal(r_s, r_s))
                link(dve.tensor_tensor(te(r_pr), te(r_ex), r_s.unsqueeze(2).broadcast_to([P, TT, NE]), ALU.mult))
                link(dve.tensor_tensor(te(r_sel), te(r_pr), brt[:, :].unsqueeze(1).broadcast_to([P, TT, NE]), ALU.add))
                rank(tge(r_sel), tge(r_rank), tge(r_g), EPG)
                link(dve.tensor_scalar(r_rank, r_rank, 2.0, None, ALU.is_lt))
                link(dve.tensor_tensor(r_g, r_sel, r_rank, ALU.mult))
                link(dve.tensor_reduce(r_gs, tge(r_g), AX.X, ALU.add))
                rank(tge(r_gs), tge(r_gr), tge(r_gg), NG)
                link(dve.tensor_scalar(r_gm, r_gr, 1.0, None, ALU.is_lt))
                link(dve.tensor_tensor(tge(r_mask), tge(r_rank), r_gm.unsqueeze(2).broadcast_to([P, TT * NG, EPG]), ALU.mult))
                link(dve.tensor_tensor(r_g, r_pr, r_mask, ALU.mult))
                steps[0] += 1
                last = dve.tensor_reduce(r_w, te(r_g), AX.X, ALU.add)
                last.then_inc(dve_step, 1)
                dve.wait_ge(dve_step, steps[0])
                link(dve.reciprocal(r_w, r_w))
                dve.tensor_tensor(te(r_g), te(r_g), r_w.unsqueeze(2).broadcast_to([P, TT, NE]), ALU.mult).then_inc(mask_ready, 1)
                dve.wait_ge(mask_ready, 1)
                dve.memset(wsel[:, :, MAXPASS * NE:], 0.0)
                dve.memset(posm[:, :, MAXPASS * NE:], -1.0)
                for r in range(MAXPASS):
                    dve.tensor_copy(wsel[:, :, NE * r:NE * r + NE], te(r_g))
                dve.wait_ge(pos_ps, 1)
                pos = PS[:, B_LOGIT + 1, 0:3 * NE]
                link(dve.scalar_tensor_tensor(out=r_sel, in0=pos[:, 0:2 * NE], scalar=1.0, in1=r_mask, op0=ALU.add, op1=ALU.mult))
                for r in range(MAXPASS):
                    last = dve.tensor_scalar(posm[:, :, NE * r:NE * r + NE], te(r_sel), -1.0 - SLOTS * r, None, ALU.add)
                link(last)
                onehots(0)
                link(dve.tensor_reduce(r_c, pos[:, 2 * NE:3 * NE], AX.X, ALU.max))
                for r in range(1, MAXPASS):
                    link(dve.tensor_scalar(r_c3[:, r - 1:r], r_c, float(SLOTS * r), float(NPAIR), ALU.is_gt, ALU.mult))
                link(dve.tensor_reduce(r_c, r_c3, AX.X, ALU.add))
                dve.tensor_scalar(n_more_t[0:1, 0:1], r_c[0:1, :], float(NPAIR - 1), None, ALU.add).then_inc(routed, 1)

            route()

            def ple_add(n):
                dve.wait_ge(sig_ready, n + 1)
                c = slice(PANEL * n, PANEL * n + PANEL)
                link(dve.tensor_tensor(sig, sig, ple[:, :, c], ALU.mult))
                dve.tensor_tensor(acc[:, :, c], acc[:, :, c], sig, ALU.add).then_inc(ple_added, 1)

            dve.wait_ge(acc_written, NP_)
            dve.wait_ge(routed, 1)
            n_more = dve.value_load(n_more_t[0:1, 0:1], min_val=NPAIR - 1, max_val=NPAIR * MAXPASS - 1)

            def spread_weights(it2):
                for e in range(2):
                    for t in range(TT):
                        last = dve.tensor_scalar(OHW[:, t, e, :], slots, posm[:, t, bass.ds(it2 + e, 1)],
                                                 wsel[:, t, bass.ds(it2 + e, 1)], ALU.is_equal, ALU.mult)
                last.then_inc(spread_ready, 1)

            def gathered_copy(it, ahead):
                dve.wait_ge(gathered, it(2, 2 * ahead + 2))
                dve.tensor_copy(XG[:, 8:16, :].rearrange("q k s -> q (k s)"),
                                PS[:, 2:4, :].rearrange("q a b -> q (a b)")).then_inc(xg_dve, 1)

            def add_sum(it, n):
                t, j = n // 4, n % 4
                a = acc[:, t, PANEL * j:PANEL * j + PANEL]
                dve.wait_ge(sum_ps, it(8, n - 7))
                dve.tensor_tensor(a, PS[:, B_Y4 + j, :], a, ALU.add).then_inc(acc_written, 1)

            gathered_copy(FIRST, 0)

            def pair_steps(it):
                if it is FIRST:
                    for u in range(PG_AHEAD, UPS):
                        for q in range(4):
                            split_lo(K_PG + u, q, K_MOE + first_at(u) + 2)
                        if u in (4, 8, 12):
                            ple_add(u // 4 - 1)
                else:
                    for n in range(8):
                        add_sum(it, n)
                for f in range(2):
                    h = HS[:, PANEL * f:PANEL * f + PANEL]
                    dve.wait_ge(weights_used, it(PAIR, 2 * UPS))
                    dve.wait_ge(silu_ready, it(2, f + 1))
                    dve.tensor_tensor(h, PS[:, B_H3 + f, :], h, ALU.mult).then_inc(h_ready, 1)
                dve.wait_ge(ht_ps, it(2, 2))
                dve.tensor_copy(HT[:, 4:8, :].rearrange("q k s -> q (k s)"), PS[:, B_H1 + 1, :]).then_inc(ht_dve, 1)
                onehots(it(2, 2))
                spread_weights(it(2, 0))
                if it is FIRST:
                    ple_add(3)
                    dve.wait_ge(ple_added, NP_)
                gathered_copy(it, 1)
                dve.wait_ge(weights_used, it(PAIR, PAIR))
                dve.tensor_copy(Y[:, 2 * PANEL:], PS[:, B_Y4 + 2:B_Y4 + 4, :].rearrange("q a b -> q (a b)")).then_inc(y_dve, 1)

            pair_steps(FIRST)
            with dve.Fori(0, n_more) as i:
                pair_steps(later(i))
            end = later(n_more)
            for n in range(8):
                add_sum(end, n)
                dve.wait_ge(acc_written, end(8, NP_ - 7 + n))
                last = dve.bn_stats(stats[:, n // 4, n % 4, :], acc[:, n // 4, PANEL * (n % 4):PANEL * (n % 4) + PANEL])
            link(last)
            layer_norm_gain(acc, 1, PIECES2, g2, ln2_in, b2, out_dve)


_INS = ["x", "p", "w_in", "w_pa", "w_pb", "w_o", "attn_sinks", "relb_table", "ln1_g", "ln1_b", "w_router", "b_router",
        "w1", "w3", "w2", "w_ple", "w_ple_gate", "ln2_g", "ln2_b", "t5_table"]


def kernel(**inputs):
    import concourse.bacc as bacc
    from concourse.bass_utils import run_bass_kernel_spmd

    nc = bacc.Bacc("TRN2", target_bir_lowering=False, num_devices=1)
    arrays, args = {}, []
    square, bucket = shape_constants()
    for name, a in [(n, inputs[n]) for n in _INS] + [("square", square), ("bucket", bucket)]:
        a = np.ascontiguousarray(a)
        arrays[f"in_{name}"] = a
        args.append(nc.dram_tensor(f"in_{name}", a.shape, mybir.dt.from_np(a.dtype), kind="ExternalInput").ap())
    out = nc.dram_tensor("out", (1, SEQ, D), F32, kind="ExternalOutput").ap()
    build(nc, *args, out)
    r = run_bass_kernel_spmd(nc, [arrays], core_ids=[0])
    return r.results[0]["out"]
```
